# Optimizing a Trainium2 kernel written in Bass

```python
import math
import jax, jax.numpy as jnp
from jax import lax
import numpy as np

D_MODEL = 1024
BATCH = 1
SEQ = 256
DEPTH = 1

DILATED_PATTERNS = ((128, 1), (512, 4), (2048, 16))
N_GROUPS = len(DILATED_PATTERNS)
HEADS_PER_GROUP = 4
N_HEADS_A = N_GROUPS * HEADS_PER_GROUP
HEAD_DIM = 128
QKV_WIDTH = N_HEADS_A * HEAD_DIM
ATTN_OUT = HEADS_PER_GROUP * HEAD_DIM
CONV_DIM = D_MODEL
CONV_WIDTH = 31
D_FF = 2816
FFN_CONV_WIDTH = 3
N_BUCKETS = 32
MAX_DISTANCE = 2048
IN_WIDTH = 3 * QKV_WIDTH + 2 * CONV_DIM + 2 * D_MODEL
RMS_EPS = 1e-6
LN_EPS = 1e-5
NEG_INF = -1e30


def rms_norm(x, g):
    xf = x.astype(jnp.float32)
    y = xf * lax.rsqrt(jnp.mean(xf * xf, axis=-1, keepdims=True) + RMS_EPS)
    return (y * g.astype(jnp.float32)).astype(x.dtype)

def layer_norm(x, g, b):
    xf = x.astype(jnp.float32)
    mu = jnp.mean(xf, axis=-1, keepdims=True)
    xc = xf - mu
    var = jnp.mean(xc * xc, axis=-1, keepdims=True)
    y = xc * lax.rsqrt(var + LN_EPS) * g.astype(jnp.float32) + b.astype(jnp.float32)
    return y.astype(x.dtype)

def causal_depthwise_conv(x, w, b):
    K, C = w.shape
    y = lax.conv_general_dilated(
        x, w[:, None, :].astype(x.dtype), window_strides=(1,), padding=[(K - 1, 0)],
        dimension_numbers=("NWC", "WIO", "NWC"), feature_group_count=C)
    return y + b.astype(x.dtype)

def t5_bucket(dist):
    max_exact = N_BUCKETS // 2
    is_small = dist < max_exact
    d = jnp.maximum(dist, 1).astype(jnp.float32)
    large = max_exact + (jnp.log(d / max_exact) / math.log(MAX_DISTANCE / max_exact)
                         * (N_BUCKETS - max_exact)).astype(jnp.int32)
    large = jnp.minimum(large, N_BUCKETS - 1)
    return jnp.where(is_small, dist, large)

def dilated_group_attention(q, k, v, bias_g, window, dilation):
    B, S, H, Dh = q.shape
    r = dilation
    span = window // dilation
    L = S // r
    nb = -(-L // span)
    Lp = nb * span

    def split(t):
        t = t.reshape(B, L, r, H, Dh).transpose(0, 2, 1, 3, 4)
        t = jnp.pad(t, ((0, 0), (0, 0), (0, Lp - L), (0, 0), (0, 0)))
        return t.reshape(B, r, nb, span, H, Dh)

    def band(t):
        prev = jnp.pad(t, ((0, 0), (0, 0), (1, 0), (0, 0), (0, 0), (0, 0)))[:, :, :-1]
        return jnp.concatenate([prev, t], axis=3)

    qb = split(q)
    kk = band(split(k))
    vv = band(split(v))

    s = jnp.einsum("brnqhd,brnkhd->brnhqk", qb, kk).astype(jnp.float32) * (Dh ** -0.5)

    qi = jnp.arange(span)[:, None]
    ki = jnp.arange(2 * span)[None, :]
    rel = qi + span - ki
    blk = jnp.arange(nb)[:, None, None]
    valid = (rel >= 0) & (rel <= span) & (blk * span + ki - span >= 0)
    bucket = t5_bucket(jnp.maximum(rel, 0) * r)
    bias = bias_g[bucket].astype(jnp.float32).transpose(2, 0, 1)

    s = jnp.where(valid[None, None, :, None], s + bias, NEG_INF)
    m = jnp.max(s, axis=-1)
    p = jnp.exp(s - m[..., None])
    l = jnp.sum(p, axis=-1)
    o = jnp.einsum("brnhqk,brnkhd->brnqhd", p, vv.astype(jnp.float32))
    m = jnp.swapaxes(m, -1, -2)
    l = jnp.swapaxes(l, -1, -2)
    o = o / l[..., None]

    def merge(t):
        t = t.reshape((B, r, Lp) + t.shape[4:])[:, :, :L]
        return jnp.swapaxes(t, 1, 2).reshape((B, S) + t.shape[3:])

    return merge(o), merge(m), merge(l)

def dilated_attention(q, k, v, rel_bias):
    outs, maxes, dens = [], [], []
    for g, (window, dilation) in enumerate(DILATED_PATTERNS):
        hs = slice(g * HEADS_PER_GROUP, (g + 1) * HEADS_PER_GROUP)
        o, m, l = dilated_group_attention(q[:, :, hs], k[:, :, hs], v[:, :, hs],
                                          rel_bias[:, hs], window, dilation)
        outs.append(o); maxes.append(m); dens.append(l)
    o = jnp.stack(outs)
    m = jnp.stack(maxes)
    l = jnp.stack(dens)
    w = l * jnp.exp(m - jnp.max(m, axis=0, keepdims=True))
    return jnp.sum(w[..., None] * o, axis=0) / jnp.sum(w, axis=0)[..., None]

def first_inputs(seed: int = 0) -> dict:
    key = jax.random.key(seed)
    ks = jax.random.split(key, 24)
    f32 = jnp.float32
    nrm = lambda k, shape, scale: jax.random.normal(k, shape, f32) * scale
    gain = lambda k, shape: 1.0 + 0.05 * jax.random.normal(k, shape, f32)
    return {
        "x": jax.random.normal(ks[0], (BATCH, SEQ, D_MODEL), f32),
        "w_in": nrm(ks[1], (DEPTH, D_MODEL, IN_WIDTH), D_MODEL ** -0.5),
        "b_gate": nrm(ks[2], (DEPTH, 2 * D_MODEL), 0.02),
        "rel_bias": nrm(ks[3], (N_BUCKETS, N_HEADS_A), 0.5),
        "w_attn_out": nrm(ks[4], (DEPTH, ATTN_OUT, D_MODEL), ATTN_OUT ** -0.5),
        "conv_dw_w": nrm(ks[5], (DEPTH, CONV_WIDTH, CONV_DIM), CONV_WIDTH ** -0.5),
        "conv_dw_b": nrm(ks[6], (DEPTH, CONV_DIM), 0.02),
        "conv_ln_g": gain(ks[7], (DEPTH, CONV_DIM)),
        "conv_ln_b": nrm(ks[8], (DEPTH, CONV_DIM), 0.02),
        "conv_pw_w": nrm(ks[9], (DEPTH, CONV_DIM, D_MODEL), CONV_DIM ** -0.5),
        "w_out": nrm(ks[10], (DEPTH, D_MODEL, D_MODEL), D_MODEL ** -0.5),
        "norm_mix_pre": gain(ks[11], (DEPTH, D_MODEL)),
        "norm_mix_post": gain(ks[12], (DEPTH, D_MODEL)),
        "norm_ffn_pre": gain(ks[13], (DEPTH, D_MODEL)),
        "norm_ffn_post": gain(ks[14], (DEPTH, D_MODEL)),
        "w_up": nrm(ks[15], (DEPTH, D_MODEL, 2 * D_FF), D_MODEL ** -0.5),
        "ffn_conv_w": nrm(ks[16], (DEPTH, FFN_CONV_WIDTH, 2 * D_FF), FFN_CONV_WIDTH ** -0.5),
        "ffn_conv_b": nrm(ks[17], (DEPTH, 2 * D_FF), 0.02),
        "w_down": nrm(ks[18], (DEPTH, D_FF, D_MODEL), D_FF ** -0.5),
    }

def first_block(x, w_in, b_gate, rel_bias, w_attn_out, conv_dw_w, conv_dw_b, conv_ln_g,
              conv_ln_b, conv_pw_w, w_out, norm_mix_pre, norm_mix_post, norm_ffn_pre,
              norm_ffn_post, w_up, ffn_conv_w, ffn_conv_b, w_down):
    B, S, D = x.shape
    for layer in range(DEPTH):
        h = rms_norm(x, norm_mix_pre[layer])
        proj = h @ w_in[layer].astype(h.dtype)
        q, k, v, glu_in, gates = jnp.split(
            proj, np.cumsum([QKV_WIDTH, QKV_WIDTH, QKV_WIDTH, 2 * CONV_DIM]).tolist(), axis=-1)
        q = q.reshape(B, S, N_HEADS_A, HEAD_DIM)
        k = k.reshape(B, S, N_HEADS_A, HEAD_DIM)
        v = v.reshape(B, S, N_HEADS_A, HEAD_DIM)

        a = dilated_attention(q, k, v, rel_bias).reshape(B, S, ATTN_OUT).astype(x.dtype)
        y_a = a @ w_attn_out[layer].astype(x.dtype)

        c_val, c_gate = jnp.split(glu_in, 2, axis=-1)
        c = c_val * jax.nn.sigmoid(c_gate)
        c = causal_depthwise_conv(c, conv_dw_w[layer], conv_dw_b[layer])
        c = jax.nn.silu(layer_norm(c, conv_ln_g[layer], conv_ln_b[layer]))
        y_c = c @ conv_pw_w[layer].astype(x.dtype)

        g = jax.nn.sigmoid(gates + b_gate[layer].astype(gates.dtype))
        g_a, g_c = jnp.split(g, 2, axis=-1)
        mixed = g_a * y_a + g_c * y_c
        out = mixed @ w_out[layer].astype(x.dtype)
        x = x + rms_norm(out, norm_mix_post[layer])

        h = rms_norm(x, norm_ffn_pre[layer])
        u = h @ w_up[layer].astype(h.dtype)
        u = causal_depthwise_conv(u, ffn_conv_w[layer], ffn_conv_b[layer])
        u_gate, u_val = jnp.split(u, 2, axis=-1)
        f = jax.nn.gelu(u_gate, approximate=True) * u_val
        y = f @ w_down[layer].astype(f.dtype)
        x = x + rms_norm(y, norm_ffn_post[layer])
    return x


CHUNK = 64
Q_BLOCK = 128

D_A = D_MODEL // 2
N_A = 64
H_A = D_A // N_A
LORA_W = max(32, int(round(1.8 * D_A ** 0.5 / 32)) * 32)
LORA_A = max(32, int(round(1.8 * D_A ** 0.5 / 32)) * 32)
LORA_G = max(32, int(round(0.6 * D_A ** 0.8 / 32)) * 32)
LNX_EPS = 64e-5

D_B = D_MODEL // 2
HD_B = 64
H_B = D_B // HD_B

D_FF_2 = ((8 * D_MODEL // 3 + 255) // 256) * 256

SHIFT_COLS = 3 * D_A + LORA_W + LORA_A + LORA_G
FOX_COLS = 3 * D_B + H_B
IN_COLS = SHIFT_COLS + FOX_COLS + 2 * D_MODEL


def rms_norm_2(x, g):
    xf = x.astype(jnp.float32)
    y = xf * lax.rsqrt(jnp.mean(xf * xf, axis=-1, keepdims=True) + RMS_EPS)
    return (y * g.astype(jnp.float32)).astype(x.dtype)

def swiglu(h, w1, w3, w2):
    return (jax.nn.silu(h @ w1) * (h @ w3)) @ w2

def token_shift(u, mu):
    prev = jnp.pad(u, ((0, 0), (1, 0), (0, 0)))[:, :-1]
    return u + (prev - u) * mu

def rwkv7_recurrence(r, w, k, v, a, b):
    B, S, H, N = r.shape
    n_chunks = S // CHUNK

    def to_chunks(t):
        return jnp.moveaxis(t, 1, 0).reshape(n_chunks, CHUNK, B, H, N)

    def step(state, inp):
        r_t, w_t, k_t, v_t, a_t, b_t = inp
        sa = jnp.einsum('bhvk,bhk->bhv', state, a_t)
        state = (state * w_t[:, :, None, :]
                 + sa[..., :, None] * b_t[:, :, None, :]
                 + v_t[..., :, None] * k_t[:, :, None, :])
        y_t = jnp.einsum('bhvk,bhk->bhv', state, r_t)
        return state, y_t

    def chunk_step(state, chunk_inp):
        return lax.scan(step, state, chunk_inp)

    xs = tuple(to_chunks(t) for t in (r, w, k, v, a, b))
    state0 = jnp.zeros((B, H, N, N), jnp.float32)
    _, ys = lax.scan(chunk_step, state0, xs)
    return jnp.moveaxis(ys.reshape(S, B, H, N), 0, 1)

def rwkv7_mixer(p, w0, w_up, a0, a_up, g_up, k_k, k_a, r_k, lnx_g, lnx_b):
    B, S, _ = p.shape
    f32 = jnp.float32
    r, k, v, w_lo, a_lo, g_lo = jnp.split(
        p, [D_A, 2 * D_A, 3 * D_A, 3 * D_A + LORA_W, 3 * D_A + LORA_W + LORA_A], axis=-1)
    w_log = -jax.nn.softplus(-(w0 + jnp.tanh(w_lo) @ w_up)) - 0.5
    decay = jnp.exp(-jnp.exp(w_log.astype(f32)))
    a = jax.nn.sigmoid(a0 + a_lo @ a_up)
    g = jax.nn.sigmoid(g_lo) @ g_up

    def heads(t):
        return t.astype(f32).reshape(B, S, H_A, N_A)

    r, k, v, a, decay = heads(r), heads(k), heads(v), heads(a), heads(decay)
    kk = k * k_k.astype(f32).reshape(H_A, N_A)
    kk = kk / jnp.maximum(jnp.sqrt(jnp.sum(kk * kk, axis=-1, keepdims=True)), 1e-12)
    k = k * (1.0 + (a - 1.0) * k_a.astype(f32).reshape(H_A, N_A))
    y = rwkv7_recurrence(r, decay, k, v, -kk, kk * a)
    mu = jnp.mean(y, axis=-1, keepdims=True)
    var = jnp.mean(jnp.square(y - mu), axis=-1, keepdims=True)
    y = ((y - mu) * lax.rsqrt(var + LNX_EPS)).reshape(B, S, D_A)
    y = y * lnx_g.astype(f32) + lnx_b.astype(f32)
    bonus = jnp.sum(r * k * r_k.astype(f32), axis=-1, keepdims=True) * v
    y = (y + bonus.reshape(B, S, D_A)) * g.astype(f32)
    return y.astype(p.dtype)

def forgetting_attention(q, k, v, log_f):
    B, H, S, hd = q.shape
    nb = S // Q_BLOCK
    scale = 1.0 / np.sqrt(hd).astype(np.float32)
    cum = jnp.cumsum(log_f, axis=-1)
    q_blocks = q.reshape(B, H, nb, Q_BLOCK, hd).transpose(2, 0, 1, 3, 4)
    c_blocks = cum.reshape(B, H, nb, Q_BLOCK).transpose(2, 0, 1, 3)
    pos_k = jnp.arange(S)

    def one_block(args):
        i, q_i, c_i = args
        s = jnp.einsum('bhqd,bhkd->bhqk', q_i, k, preferred_element_type=jnp.float32) * scale
        s = s + c_i[..., :, None] - cum[..., None, :]
        pos_q = i * Q_BLOCK + jnp.arange(Q_BLOCK)
        mask = pos_k[None, :] <= pos_q[:, None]
        s = jnp.where(mask, s, -jnp.inf)
        pr = jax.nn.softmax(s, axis=-1)
        return jnp.einsum('bhqk,bhkd->bhqd', pr.astype(v.dtype), v)

    out = lax.map(one_block, (jnp.arange(nb), q_blocks, c_blocks))
    return out.transpose(1, 2, 0, 3, 4).reshape(B, H, S, hd)

def fox_mixer(p, f_bias, q_norm, k_norm):
    B, S, _ = p.shape
    q, k, v, f_lo = jnp.split(p, [D_B, 2 * D_B, 3 * D_B], axis=-1)

    def heads(t):
        return t.reshape(B, S, H_B, HD_B).transpose(0, 2, 1, 3)

    q = rms_norm_2(heads(q), q_norm)
    k = rms_norm_2(heads(k), k_norm)
    v = heads(v)
    log_f = jax.nn.log_sigmoid((f_lo + f_bias).astype(jnp.float32)).transpose(0, 2, 1)
    o = forgetting_attention(q, k, v, log_f)
    return o.transpose(0, 2, 1, 3).reshape(B, S, D_B)

def second_inputs(seed: int = 0) -> dict:
    key = jax.random.key(seed)
    ks = jax.random.split(key, 28)
    L = DEPTH
    f32 = jnp.float32

    def nrm(k, shape, scale):
        return jax.random.normal(k, shape, f32) * scale

    def gain(k, shape):
        return 1.0 + 0.05 * jax.random.normal(k, shape, f32)

    return {
        "x": nrm(ks[0], (BATCH, SEQ, D_MODEL), 1.0),
        "ffn1_norm": gain(ks[1], (L, D_MODEL)),
        "ffn1_w1": nrm(ks[2], (L, D_MODEL, D_FF_2), D_MODEL ** -0.5),
        "ffn1_w3": nrm(ks[3], (L, D_MODEL, D_FF_2), D_MODEL ** -0.5),
        "ffn1_w2": nrm(ks[4], (L, D_FF_2, D_MODEL), D_FF_2 ** -0.5),
        "mix_norm": gain(ks[5], (L, D_MODEL)),
        "w_in": nrm(ks[6], (L, D_MODEL, IN_COLS), D_MODEL ** -0.5),
        "shift_mu": jax.random.uniform(ks[7], (L, SHIFT_COLS), f32),
        "rwkv_w0": jax.random.uniform(ks[8], (L, D_A), f32, -6.5, -1.5),
        "rwkv_w_up": nrm(ks[9], (L, LORA_W, D_A), 0.5 * LORA_W ** -0.5),
        "rwkv_a0": nrm(ks[10], (L, D_A), 0.1),
        "rwkv_a_up": nrm(ks[11], (L, LORA_A, D_A), LORA_A ** -0.5),
        "rwkv_g_up": nrm(ks[12], (L, LORA_G, D_A), LORA_G ** -0.5),
        "rwkv_k_k": 0.85 + 0.05 * jax.random.normal(ks[13], (L, D_A), f32),
        "rwkv_k_a": gain(ks[14], (L, D_A)),
        "rwkv_r_k": nrm(ks[15], (L, H_A, N_A), 0.1),
        "rwkv_lnx_g": gain(ks[16], (L, D_A)),
        "rwkv_lnx_b": nrm(ks[17], (L, D_A), 0.02),
        "rwkv_proj": nrm(ks[18], (L, D_A, D_MODEL), D_A ** -0.5),
        "fox_f_bias": 2.0 + 0.5 * jax.random.normal(ks[19], (L, H_B), f32),
        "fox_q_norm": gain(ks[20], (L, HD_B)),
        "fox_k_norm": gain(ks[21], (L, HD_B)),
        "fox_proj": nrm(ks[22], (L, D_B, D_MODEL), D_B ** -0.5),
        "w_out": nrm(ks[23], (L, D_MODEL, D_MODEL), D_MODEL ** -0.5),
        "ffn2_norm": gain(ks[24], (L, D_MODEL)),
        "ffn2_w1": nrm(ks[25], (L, D_MODEL, D_FF_2), D_MODEL ** -0.5),
        "ffn2_w3": nrm(ks[26], (L, D_MODEL, D_FF_2), D_MODEL ** -0.5),
        "ffn2_w2": nrm(ks[27], (L, D_FF_2, D_MODEL), D_FF_2 ** -0.5),
        "final_norm": gain(jax.random.fold_in(key, 99), (D_MODEL,)),
    }

def second_block(x, ffn1_norm, ffn1_w1, ffn1_w3, ffn1_w2, mix_norm, w_in, shift_mu,
              rwkv_w0, rwkv_w_up, rwkv_a0, rwkv_a_up, rwkv_g_up, rwkv_k_k, rwkv_k_a, rwkv_r_k,
              rwkv_lnx_g, rwkv_lnx_b, rwkv_proj, fox_f_bias, fox_q_norm, fox_k_norm, fox_proj,
              w_out, ffn2_norm, ffn2_w1, ffn2_w3, ffn2_w2, final_norm):
    for l in range(DEPTH):
        x = x + 0.5 * swiglu(rms_norm_2(x, ffn1_norm[l]), ffn1_w1[l], ffn1_w3[l], ffn1_w2[l])

        h = rms_norm_2(x, mix_norm[l])
        p = h @ w_in[l]
        p_rwkv = token_shift(p[..., :SHIFT_COLS], shift_mu[l])
        p_fox = p[..., SHIFT_COLS:SHIFT_COLS + FOX_COLS]
        gates = jax.nn.sigmoid(p[..., SHIFT_COLS + FOX_COLS:])
        gate_a, gate_b = gates[..., :D_MODEL], gates[..., D_MODEL:]

        y_a = rwkv7_mixer(p_rwkv, rwkv_w0[l], rwkv_w_up[l], rwkv_a0[l], rwkv_a_up[l], rwkv_g_up[l],
                          rwkv_k_k[l], rwkv_k_a[l], rwkv_r_k[l], rwkv_lnx_g[l], rwkv_lnx_b[l]) @ rwkv_proj[l]
        y_b = fox_mixer(p_fox, fox_f_bias[l], fox_q_norm[l], fox_k_norm[l]) @ fox_proj[l]
        x = x + (gate_a * y_a + gate_b * y_b) @ w_out[l]

        x = x + 0.5 * swiglu(rms_norm_2(x, ffn2_norm[l]), ffn2_w1[l], ffn2_w3[l], ffn2_w2[l])
    return rms_norm_2(x, final_norm)


def setup_inputs(seed=0):
    out = dict(first_inputs(seed))
    for name, value in second_inputs(seed + 1).items():
        if name != "x":
            out[name + "_2"] = value
    return out


def reference(
    x, w_in, b_gate, rel_bias, w_attn_out, conv_dw_w, conv_dw_b, conv_ln_g, conv_ln_b,
    conv_pw_w, w_out, norm_mix_pre, norm_mix_post, norm_ffn_pre, norm_ffn_post, w_up,
    ffn_conv_w, ffn_conv_b, w_down, ffn1_norm_2, ffn1_w1_2, ffn1_w3_2, ffn1_w2_2, mix_norm_2,
    w_in_2, shift_mu_2, rwkv_w0_2, rwkv_w_up_2, rwkv_a0_2, rwkv_a_up_2, rwkv_g_up_2, rwkv_k_k_2,
    rwkv_k_a_2, rwkv_r_k_2, rwkv_lnx_g_2, rwkv_lnx_b_2, rwkv_proj_2, fox_f_bias_2, fox_q_norm_2,
    fox_k_norm_2, fox_proj_2, w_out_2, ffn2_norm_2, ffn2_w1_2, ffn2_w3_2, ffn2_w2_2,
    final_norm_2,
):
    x = first_block(
        x, w_in, b_gate, rel_bias, w_attn_out, conv_dw_w, conv_dw_b, conv_ln_g, conv_ln_b,
        conv_pw_w, w_out, norm_mix_pre, norm_mix_post, norm_ffn_pre, norm_ffn_post, w_up,
        ffn_conv_w, ffn_conv_b, w_down,
    )
    return second_block(
        x, ffn1_norm_2, ffn1_w1_2, ffn1_w3_2, ffn1_w2_2, mix_norm_2, w_in_2, shift_mu_2,
        rwkv_w0_2, rwkv_w_up_2, rwkv_a0_2, rwkv_a_up_2, rwkv_g_up_2, rwkv_k_k_2, rwkv_k_a_2,
        rwkv_r_k_2, rwkv_lnx_g_2, rwkv_lnx_b_2, rwkv_proj_2, fox_f_bias_2, fox_q_norm_2,
        fox_k_norm_2, fox_proj_2, w_out_2, ffn2_norm_2, ffn2_w1_2, ffn2_w3_2, ffn2_w2_2,
        final_norm_2,
    )


_drawn_inputs = setup_inputs


def setup_inputs(seed=0):
    import zlib

    import numpy as np

    out = dict(_drawn_inputs(seed))
    spreads = {}
    factors = {'b_gate': 7.942,
     'conv_ln_b': 3.286,
     'ffn_conv_b': 3.199,
     'ffn1_norm_2': 4.361,
     'mix_norm_2': 3.067,
     'rwkv_w_up_2': 8.0,
     'rwkv_a0_2': 8.0,
     'rwkv_k_k_2': 53.776,
     'rwkv_k_a_2': 6.026,
     'rwkv_lnx_g_2': 33.593,
     'rwkv_lnx_b_2': 64.0,
     'fox_f_bias_2': 2.793,
     'fox_q_norm_2': 8.0,
     'fox_k_norm_2': 8.0,
     'ffn2_norm_2': 4.808}
    for name, (base, spread) in spreads.items():
        noise = np.random.default_rng([zlib.crc32(name.encode()), seed]).standard_normal(out[name].shape)
        drawn = base * np.exp(spread * noise) if base else spread * noise
        out[name] = __import__('jax').numpy.asarray(drawn.astype(out[name].dtype))
    for name, factor in factors.items():
        out[name] = (out[name] * factor).astype(out[name].dtype)
    return out
```

```python
import math
from contextlib import ExitStack

import numpy as np

import concourse.bass as bass
from concourse import mybir

F32 = mybir.dt.float32
F32R = mybir.dt.float32r
ALU = mybir.AluOpType
ACT = mybir.ActivationFunctionType
AX = mybir.AxisListType

P = 128
T = 256
TT = T // P
D = 1024
NT = D // P
HEAD = 128
GROUPS = 3
HPG = 4
QKV = GROUPS * HPG * HEAD
DILATION = (1, 4, 16)
SPAN = 128
BUCKETS = 32
MAX_DIST = 2048
CONV_W = 31
PAD = CONV_W - 1
FF = 2816
FT = FF // P
FPAIRS = FT // 2
NEG = -1e30
HALF = 512
HT = HALF // P
HD = 64
NH = HALF // HD
CHUNK = 64
NCH = T // CHUNK
LORA = 160
SHIFT = 3 * HALF + LORA
FOX = SHIFT + 3 * HALF
GATES_2 = FOX + NH
RING = 3
CW = 2048
LO_DVE = 512


def bucket_runs():
    exact = BUCKETS // 2
    runs = []
    for d in range(exact, T):
        f = np.float32(np.log(np.float32(d) / np.float32(exact)))
        b = min(exact + int(f / np.float32(math.log(MAX_DIST / exact)) * np.float32(BUCKETS - exact)), BUCKETS - 1)
        if runs and runs[-1][0] == b:
            runs[-1][2] = d
        else:
            runs.append([b, d, d])
    return runs


class Signals:

    def __init__(self, nc, ctx):
        self.nc, self.ctx, self.by_name = nc, ctx, {}

    def __getitem__(self, name):
        if name not in self.by_name:
            self.by_name[name] = self.ctx.enter_context(self.nc.semaphore(name))
        return self.by_name[name]


def due(value):
    return not isinstance(value, int) or value > 0


class Count:

    def __init__(self):
        self.count, self.i, self.per = {}, None, {}

    def value(self, name):
        n = self.count.get(name, 0)
        return n if self.i is None or name not in self.per else self.i * self.per[name] + n

    def one(self, name):
        self.count[name] = self.count.get(name, 0) + 1
        return 1

    def enter(self, i, per):
        self.i, self.per, self.start = i, per, dict(self.count)

    def leave(self, times):
        for name, n in self.count.items():
            began = self.start.get(name, 0)
            assert n - began == self.per.get(name, 0), (name, n - began)
            self.count[name] = began + (n - began) * times
        self.i, self.per = None, {}


def block_pair(nc, inp, out, scratch, shifted):
    ctx = ExitStack()
    with ctx:
        S = Signals(nc, ctx)

        def sb(name, shape, dt=F32):
            return ctx.enter_context(nc.sbuf_tensor(name, shape, dt))

        bank = [ctx.enter_context(nc.psum_tensor(f"bank{b}", [P, 512], F32)) for b in range(8)]
        raw = [sb(f"w_raw{s}", [P, CW]) for s in range(RING)]
        w_hi = [sb(f"w_hi{s}", [P, CW], F32R) for s in range(RING)]
        w_lo = [sb(f"w_lo{s}", [P, CW], F32R) for s in range(RING)]
        X_hi, X_lo = sb("X_hi", [P, NT, T], F32R), sb("X_lo", [P, NT, T], F32R)
        Y_hi, Y_lo = sb("Y_hi", [P, NT, T], F32R), sb("Y_lo", [P, NT, T], F32R)
        x = sb("x", [P, NT, T])
        sq = sb("sq", [P, 4, 512])
        ident, ones, head_ones = sb("ident", [P, P]), sb("ones", [P, P]), sb("head_ones", [P, P])
        zeros_r = sb("zeros_r", [P, 512], F32R)
        par = sb("par", [P, 5 * P])
        eps = sb("eps", [P, 4])
        rcol, rstd, diag = sb("rcol", [P, 4]), sb("rstd", [P, T]), sb("diag", [P, TT, P])
        ARENA = 18700
        arena = sb("arena", [P, ARENA])

        def region(at, *shape):
            n = int(np.prod(shape))
            assert at + n <= ARENA
            v = arena[:, at:at + n]
            if len(shape) == 2:
                v = v.rearrange("p (a b) -> p a b", a=shape[0])
            if len(shape) == 3:
                v = v.rearrange("p (a b c) -> p a b c", a=shape[0], b=shape[1])
            return v

        def flat(v):
            return v.rearrange("p a b -> p (a b)")

        def pairs(b):
            return bank[b][:, :].rearrange("p (m t) -> p m t", m=2)

        def over(v, n):
            return v[:, None, :].to_broadcast([P, n, v.shape[1]])

        rows, staged = {}, []

        def stage(name, group, row, ap, lo=0):
            rows[name] = group * P + row
            staged.append((group, row, lo, ap))

        at = 0
        for name in ("norm_mix_pre", "norm_mix_post", "norm_ffn_pre", "norm_ffn_post", "b_gate", "conv_dw_b",
                     "conv_ln_g", "conv_ln_b", "ffn1_norm_2", "mix_norm_2", "ffn2_norm_2", "final_norm_2",
                     "rwkv_w0_2", "rwkv_a0_2", "rwkv_k_k_2", "rwkv_k_a_2"):
            v = inp[name] if name == "final_norm_2" else inp[name].rearrange("a d -> (a d)")
            stage(name, 0, at, v.rearrange("(r c) -> r c", c=P))
            at += v.shape[0] // P
        assert at <= P
        at = 0
        for name, v in (("rwkv_r_k_2", inp["rwkv_r_k_2"].rearrange("a h d -> (a h d)")),
                        ("rwkv_lnx_g_2", inp["rwkv_lnx_g_2"].rearrange("a d -> (a d)")),
                        ("rwkv_lnx_b_2", inp["rwkv_lnx_b_2"].rearrange("a d -> (a d)")),
                        ("mu", inp["shift_mu_2"][0, 0:3 * HALF + P]),
                        ("ffn_conv_b", inp["ffn_conv_b"].rearrange("a d -> (a d)"))):
            stage(name, 1, at, v.rearrange("(r c) -> r c", c=P))
            at += v.shape[0] // P
        stage("mu_tail", 1, at, inp["shift_mu_2"][:, 3 * HALF + P:SHIFT])
        for h in range(2):
            stage("fox_q_norm_2", 1, at + 1, inp["fox_q_norm_2"], HD * h)
            stage("fox_k_norm_2", 1, at + 2, inp["fox_k_norm_2"], HD * h)
        stage("fox_f_bias_2", 1, at + 3, inp["fox_f_bias_2"], 32)
        assert at + 4 <= P
        at = 2 * P
        for name in ("ffn_conv_w", "conv_dw_w"):
            v = inp[name].rearrange("a k (r c) -> (a k r) c", c=P)
            first, done = at, 0
            while done < v.shape[0]:
                n = min(P - at % P, v.shape[0] - done)
                stage(name, at // P, at % P, v[done:done + n, :])
                at, done = at + n, done + n
            rows[name] = first
        assert at <= 5 * P

        def col(name, t=0, lo=0, hi=P):
            return par[lo:hi, rows[name] + t:rows[name] + t + 1]

        def col_chunk(w, c0, width=256):
            return w[0, :, c0:c0 + width].rearrange("(k p) c -> p k c", p=P)

        def row_chunk(w, r):
            return w[0, r * 2 * P:(r + 1) * 2 * P, :].rearrange("(k p) c -> p k c", p=P)

        chunks = []

        def add(*parts):
            chunks.append(parts)

        w_in, w_in_2 = inp["w_in"], inp["w_in_2"]
        GLU, GATES = 3 * QKV, 3 * QKV + 2 * D
        for j in range(4):
            add((col_chunk(w_in, GLU + 256 * j), 0))
            add((col_chunk(w_in, GLU + D + 256 * j), 0))
        A_QKV = len(chunks)
        for j in range(3 * QKV // 256):
            add((col_chunk(w_in, 256 * j), 0))
        A_GA = len(chunks)
        for j in range(4):
            add((col_chunk(w_in, GATES + 256 * j), 0))
        for j in range(4):
            add((col_chunk(w_in, GATES + D + 256 * j), 0))
        A_AO = len(chunks)
        for r in range(2):
            add((row_chunk(inp["w_attn_out"], r), 0))
        A_PW = len(chunks)
        PW_ROWS = (2, 3, 0, 1)
        for r in PW_ROWS:
            add((row_chunk(inp["conv_pw_w"], r), 0))
        A_WO = len(chunks)
        for r in range(4):
            add((row_chunk(inp["w_out"], r), 0))
        A_END = len(chunks)

        def feed_forward(gate, val, down):
            b0 = len(chunks)
            add((gate(0), 0))
            add((val(0), 0))
            for i in range(FPAIRS):
                if i + 1 < FPAIRS:
                    add((gate(i + 1), 0))
                    add((val(i + 1), 0))
                add((down(i), 0))
            return b0

        def ffn_sources(k):
            if k == 0:
                g, v, d = inp["w_up"], inp["w_up"], inp["w_down"]
                off = FF
            else:
                g, v, d = inp[f"ffn{k}_w1_2"], inp[f"ffn{k}_w3_2"], inp[f"ffn{k}_w2_2"]
                off = 0
            return g, v, d, off

        def gate_source(k, i):
            g, _, _, _ = ffn_sources(k)
            return g.rearrange("a (k p) c -> p (a k) c", p=P)[:, :, bass.ds(i * 256, 256)]

        def val_source(k, i):
            _, v, _, off = ffn_sources(k)
            return v.rearrange("a (k p) c -> p (a k) c", p=P)[:, :, bass.ds(i * 256 + off, 256)]

        def down_source(k, i):
            _, _, d, _ = ffn_sources(k)
            return d.rearrange("a (k p) c -> p (a k) c", p=P)[:, bass.ds(i * 2, 2), :]

        ffn_at = {}
        for k in (0, 1):
            ffn_at[k] = feed_forward(lambda i: gate_source(k, i), lambda i: val_source(k, i),
                                     lambda i: down_source(k, i))
        B0 = len(chunks)
        add((col_chunk(w_in_2, 3 * HALF, LORA), 0), (col_chunk(w_in_2, FOX, 256 - LORA), LORA))
        KRV = (2, 3, 0, 1, 4, 5)
        for j in KRV:
            add((col_chunk(w_in_2, 256 * j), 0))
        B_FOX = len(chunks)
        for j in range(6):
            add((col_chunk(w_in_2, SHIFT + 256 * j), 0))
        B_GA = len(chunks)
        for j in range(8):
            add((col_chunk(w_in_2, GATES_2 + 256 * j), 0))
        B_RP = len(chunks)
        for r in range(2):
            add((row_chunk(inp["rwkv_proj_2"], r), 0))
        B_FP = len(chunks)
        for r in range(2):
            add((row_chunk(inp["fox_proj_2"], r), 0))
        B_WO = len(chunks)
        for r in range(4):
            add((row_chunk(inp["w_out_2"], r), 0))
        ffn_at[2] = feed_forward(lambda i: gate_source(2, i), lambda i: val_source(2, i),
                                 lambda i: down_source(2, i))
        TOTAL = len(chunks)
        LAYER_ENDS = (A_END, ffn_at[1], B0, ffn_at[2], TOTAL)
        landed, used = [], [0] * RING
        for n, parts in enumerate(chunks):
            used[n % RING] += 16 * len(parts)
            landed.append(used[n % RING])

        q_t, k_t = region(0, GROUPS * HPG, T), region(3072, GROUPS * HPG, T)
        v_t = region(6144, TT, QKV)
        c_pad = region(9216, NT, PAD + T)
        s_t = region(9216, 2, 768)
        pT = region(9216 + 1536, 768)
        conv = region(11520, NT, T)
        gate_a = region(13568, NT, T)
        bias_t = region(15616, GROUPS * HPG, T)
        gate_c = sq[:, :, :].rearrange("p q (m t) -> p (q m) t", m=2)
        mixed_a = region(3072, NT, T)
        onehot = region(13568, T)
        table = region(13568 + 256, GROUPS, 384)
        heads = region(13568 + 1408, 16)
        x_in = region(0, TT, D)
        par_in = region(2048, 5, P)
        u_t = region(0, 2, 2 * T)
        acc = region(1024, 2, 2, T)
        act_t, f_t = region(2048, 2 * T), region(2560, 2 * T)
        xg = region(4096, NT, T)
        out_t = region(6144, TT, D)

        glu = region(3072, 2, 2, 2 * T)
        tmp = region(6144, 2 * T)
        ar = region(0, NCH * HT, 2 * CHUNK)
        bonus, g_out = region(2048, HT, T), region(3072, HT, T)
        b_dec, k_dec = region(4096, HT, T), region(5120, HT, T)
        r_s, k_s, v_s = region(6144, HT, T), region(7168, HT, T), region(8192, HT, T)
        kk, rate = region(9216, HT, T), region(10240, HT, T)
        dec_prev, dec_inv, dec = region(11264, HT, T), region(12288, HT, T), region(13312, HT, T)
        unshifted = region(14336, 4, T + 1)
        lora_in = region(15364, 2, T + 1)
        lora_act = region(15878, 2, T)
        lora_w = region(16390, 2, HALF)
        early = region(17414, HT, T)
        forget = region(18440, T)
        x_inv, xt_inv = region(4096, NCH * HT, CHUNK), region(5120, NCH * HT, CHUNK)
        m_b, m_k = region(6144, NCH * HT, 2 * CHUNK), region(9216, NCH * HT, 2 * CHUNK)
        b_tok, k_tok, v_tok = (region(11264 + 1024 * j, NCH * HT, CHUNK) for j in range(3))
        half_1, half_n = region(14336, 2, 8 * CHUNK), region(15360, 2, 8 * CHUNK)
        y_t = region(14336, HT, T)
        state_t, w_s, sa_s = (region(15360 + 256 * j, HT, CHUNK) for j in range(3))
        fq, fk = region(16384, HT, T), region(17408, HT, T)
        fv = region(8192, TT, HALF)
        late, late_sq = region(4096, HT, T), region(5120, HT, T)
        gate_2a, gate_2b = region(6144, NT, T), region(9216, NT, T)
        fs_t, fpT = region(11264, 2, 512), region(12288, 512)
        mask_2 = sb("mask_2", [P, 2 * CHUNK])
        levels = sb("levels", [P, 6, CHUNK])
        eye = sb("eye", [P, CHUNK])
        resets = sb("resets", [P, T])
        causal = sb("causal", [P, T])
        small = sb("small", [P, 68])

        bank_of, reads, times = {}, {}, [0] * 3
        for n in [*range(A_AO), *range(B0, B_RP)]:
            bank_of[n] = n % 3
            times[n % 3] += 1
            reads[n] = times[n % 3]

        def all_read(before):
            return [max([0] + [reads[n] for n in reads if n < before and bank_of[n] == b]) for b in range(3)]


        EXP_HALF = math.exp(-0.5)
        LEVELS = 5
        FUNITS = HT * TT
        nmax = small[:, 0:4].rearrange("p (b h) -> p b h", b=2)
        den = small[:, 64:68].rearrange("p (b h) -> p b h", b=2)
        rden = small[:, 4:6]
        forget_col = small[:, 8:24].rearrange("p (t h) -> p t h", t=TT)
        dec_end = small[:, 24:40].rearrange("p (t c) -> p t c", t=HT)
        head_col, kept, q_gain = small[:, 40:56], small[:, 56:60], small[:, 60:61]

        def second_constants(told, pool, g):
            g.memset(mask_2[:], 1.0).then_inc(S["pool_step"], told.one("pool_step"))
            g.memset(levels[:], 0.0).then_inc(S["pool_step"], told.one("pool_step"))
            g.memset(resets[:], 1.0).then_inc(S["pool_step"], told.one("pool_step"))
            g.memset(causal[:], 0.0).then_inc(S["pool_step"], told.one("pool_step"))
            pool.wait_ge(S["pool_step"], told.value("pool_step"))
            g.memset(resets[:, 0:T:CHUNK], 0.0).then_inc(S["pool_step"], told.one("pool_step"))
            g.affine_select(out=causal[:], in_=causal[:], compare_op=ALU.is_ge, fill=NEG, base=P,
                            pattern=[[-1, T]], channel_multiplier=1).then_inc(S["pool_step"], told.one("pool_step"))
            pool.wait_ge(S["pool_step"], told.value("pool_step"))
            for h in range(2):
                a, b = HD * h, HD * (h + 1)
                g.tensor_copy(eye[a:b, :], ident[a:b, a:b]).then_inc(S["pool_step"], told.one("pool_step"))
                pool.wait_ge(S["pool_step"], told.value("pool_step"))
                for k in range(2):
                    v = mask_2[a:b, k * CHUNK:(k + 1) * CHUNK]
                    g.affine_select(out=v, in_=v, compare_op=ALU.is_ge, fill=0.0, base=k - 1,
                                    pattern=[[1, CHUNK]], channel_multiplier=-1).then_inc(
                        S["pool_step"], told.one("pool_step"))
                    pool.wait_ge(S["pool_step"], told.value("pool_step"))
            for n in range(LEVELS + 1):
                w = 2 ** n
                both = levels[:, n, :].rearrange("p (b t) -> p b t", t=2 * w)
                g.memset(both[:, :, w:2 * w], 1.0).then_inc(S["pool_step"], told.one("pool_step"))
                pool.wait_ge(S["pool_step"], told.value("pool_step"))
                for h in range(2):
                    v = both[HD * h:HD * (h + 1)]
                    blocks = CHUNK // (2 * w)
                    g.affine_select(out=v, in_=v, compare_op=ALU.is_ge, fill=0.0, base=0,
                                    pattern=[[-2 * w, blocks], [0, 2 * w]], channel_multiplier=1).then_inc(
                        S["pool_step"], told.one("pool_step"))
                    pool.wait_ge(S["pool_step"], told.value("pool_step"))
                    done = "masks_ready" if n == LEVELS and h else "pool_step"
                    g.affine_select(out=v, in_=v, compare_op=ALU.is_ge, fill=0.0, base=w - 1,
                                    pattern=[[2 * w, blocks], [0, 2 * w]], channel_multiplier=-1).then_inc(
                        S[done], told.one(done))
                    pool.wait_ge(S[done], told.value(done))

        def by_chunk(v):
            return v.rearrange("p t (c s) -> p t c s", c=NCH)

        def ar_part(k):
            return ar.rearrange("p (c t) (k s) -> p t c k s", c=NCH, k=2)[:, :, :, k, :]

        def head(v, h, *rest):
            return v[(slice(HD * h, HD * (h + 1)), *rest)]

        def pe_mixer(told, pe, state, by_columns, by_tokens, by_rows, sum_squares, spread):
            def columns(n, fresh=False, tokens=False):
                pe.wait_ge(S[f"bank{bank_of[n]}_read"], reads[n] - 1)
                if tokens:
                    by_tokens(n, n % RING, bank_of[n])
                else:
                    by_columns(n, n % RING, bank_of[n], fresh=fresh)

            def to_tokens(src, c, t, h, o):
                return pe.matmul(o, head(src, h, t, slice(c * CHUNK, (c + 1) * CHUNK)),
                                 head(ident, h, slice(HD * h, HD * (h + 1))), start=True, stop=True)

            def all_to_tokens(src, b):
                for c in range(NCH):
                    for t in range(HT):
                        u = c * HT + t
                        for h in range(2):
                            mm = to_tokens(src, c, t, h, head(bank[b + u // 8], h, slice(u % 8 * CHUNK, u % 8 * CHUNK + CHUNK)))
                return mm

            def head_sums(src):
                for tt in range(TT):
                    for t in range(HT):
                        o = 256 + (tt * HT + t) * 2
                        mm = pe.matmul(bank[3][:, o:o + 2], src[:, t, tt * P:(tt + 1) * P], head_ones[:, 0:P:HD],
                                       start=True, stop=True)
                mm.then_inc(S["head_sums"], told.one("head_sums"))

            def turn_factors(src, b):
                for t in range(HT):
                    for tt in range(TT):
                        mm = pe.transpose(bank[b + t // 2][:, t % 2 * T + tt * P:t % 2 * T + (tt + 1) * P],
                                          src[:, 2 * tt + t // 2, t % 2 * P:(t % 2 + 1) * P], ident[:])
                mm.then_inc(S["factors_turned"], told.one("factors_turned"))

            columns(B0, fresh=True)
            sum_squares()
            spread()
            columns(B0 + 1)
            pe.wait_ge(S["lora_landed"], 64)
            pe.wait_ge(S["lora_act"], 3)
            for t in range(HT):
                mm = pe.matmul(bank[6 + t // 2][:, t % 2 * T:t % 2 * T + T], lora_w[0:32, 0, t * P:(t + 1) * P],
                               lora_act[0:32, 0, :], start=True, stop=True)
            mm.then_inc(S["decay_in"], told.one("decay_in"))
            for t in range(HT):
                mm = pe.matmul(bank[4 + t // 2][:, t % 2 * T:t % 2 * T + T], lora_w[32:64, 0, t * P:(t + 1) * P],
                               lora_act[32:64, 0, :], start=True, stop=True)
            mm.then_inc(S["rate_in"], told.one("rate_in"))
            columns(B0 + 2)
            columns(B0 + 3)
            pe.wait_ge(S["kk_squared"], 1)
            pe.wait_ge(S["rstd"], state["rstd"])
            head_sums(early)
            pe.wait_ge(S["decay_read"], HT)
            for t in range(HT):
                o = bank[6 + t // 2][:, t % 2 * T:t % 2 * T + T]
                pe.matmul(o, lora_w[64:128, 0, t * P:(t + 1) * P], lora_act[64:128, 0, :], start=True, stop=False)
                mm = pe.matmul(o, lora_w[0:32, 1, t * P:(t + 1) * P], lora_act[0:32, 1, :], start=False, stop=True)
            mm.then_inc(S["gate_in"], told.one("gate_in"))
            columns(B0 + 4)
            pe.wait_ge(S["rate_read"], HT)
            pe.wait_ge(S["factors"], 1)
            turn_factors(early, 4)
            columns(B0 + 5)
            pe.wait_ge(S["forget"], 1)
            for tt in range(TT):
                mm = pe.matmul(bank[3][:, 256 + tt * NH:256 + (tt + 1) * NH], forget[32:32 + NH, tt * P:(tt + 1) * P],
                               ident[32:32 + NH, 32:32 + NH], start=True, stop=True)
            mm.then_inc(S["forget_turned"], told.one("forget_turned"))
            columns(B0 + 6)
            columns(B_FOX)
            pe.wait_ge(S["g_read"], 2)
            pe.wait_ge(S["rk_ready"], 1)
            for t in range(HT):
                mm = pe.matmul(bank[6 + t // 2][:, t % 2 * T:t % 2 * T + T], head_ones[:, :], early[:, t, :],
                               start=True, stop=True)
            mm.then_inc(S["bonus_in"], told.one("bonus_in"))
            columns(B_FOX + 1)
            pe.wait_ge(S["decayed"], 1)
            for c in range(NCH):
                if 2 * c > 0:
                    pe.wait_ge(S["masked"], 2 * c)
                for src, b in ((b_dec, 4), (k_dec, 5)):
                    for t in range(HT):
                        for h in range(2):
                            mm = pe.matmul(head(bank[b], h, slice(t * P, (t + 1) * P)),
                                           head(src, h, t, slice(c * CHUNK, (c + 1) * CHUNK)),
                                           head(ar, h, c * HT + t), start=True, stop=True)
                    mm.then_inc(S["chunk_scores"], told.one("chunk_scores"))
            all_to_tokens(b_dec, 6).then_inc(S["b_turned"], told.one("b_turned"))
            pe.wait_ge(S["masked"], 2 * NCH)
            all_to_tokens(k_dec, 4).then_inc(S["k_turned"], told.one("k_turned"))
            pe.wait_ge(S["b_tok"], 2)
            all_to_tokens(v_s, 6).then_inc(S["v_turned"], told.one("v_turned"))
            pe.wait_ge(S["xt_first"], 1)
            pe.wait_ge(S["k_tok"], 2)
            for u in range(NCH * HT):
                for h in range(2):
                    mm = pe.matmul(head(bank[4 + u // 8], h, slice(u % 8 * CHUNK, u % 8 * CHUNK + CHUNK)),
                                   head(xt_inv, h, u), head(ident, h, slice(HD * h, HD * (h + 1))),
                                   start=True, stop=True)
            mm.then_inc(S["x_first"], told.one("x_first"))
            for n in range(1, LEVELS + 1):
                def product(b, left, right, f):
                    for i in range(8):
                        for h in range(2):
                            mm = pe.matmul(head(bank[b], h, slice(i * CHUNK, (i + 1) * CHUNK)), left(f, i, h),
                                           right(f, i, h), start=True, stop=True)
                    return mm

                def x_of(f, i, h):
                    return head(x_inv, h, 8 * f + i)

                def xt_of(f, i, h):
                    return head(xt_inv, h, 8 * f + i)

                def n_of(f, i, h):
                    return head(half_n, h, f, slice(i * CHUNK, (i + 1) * CHUNK))

                def p_of(f, i, h):
                    return head(half_1, h, f, slice(i * CHUNK, (i + 1) * CHUNK))

                pe.wait_ge(S["x_copied"], 2)
                pe.wait_ge(S["v_tok"], 2)
                for f in range(2):
                    pe.wait_ge(S["off_ready"], 2 * (n - 1) + f + 1)
                    if 2 * (n - 1) - 1 + f > 0:
                        pe.wait_ge(S["xt_added"], 2 * (n - 1) - 1 + f)
                    product(4 + f, n_of, x_of, f).then_inc(S["p1"], told.one("p1"))
                for f in range(2):
                    if f and n > 1:
                        columns(B_FOX + n, tokens=n >= 4)
                    pe.wait_ge(S["p1_copied"], 2 * (n - 1) + f + 1)
                    if 2 * (n - 1) + f > 0:
                        pe.wait_ge(S["xt_added"], 2 * (n - 1) + f)
                    if n < LEVELS:
                        product(6, xt_of, p_of, f)
                    product(7, p_of, xt_of, f).then_inc(S["p2"], told.one("p2"))
            for c in range(NCH):
                def each(fn):
                    for t in range(HT):
                        for h in range(2):
                            mm = fn(t, h, c * HT + t)
                    return mm

                def cell(b, t, h):
                    return head(bank[b], h, slice(t * CHUNK, (t + 1) * CHUNK))

                def mul(o, left, right, start, stop):
                    return pe.matmul(o, left, right, start=start, stop=stop, skip_group_check=True)

                def decayed(k, u, h):
                    return head(ar, h, u, slice(k * CHUNK, (k + 1) * CHUNK))

                pe.wait_ge(S["xt_added"], 2 * LEVELS)
                if c > 0:
                    pe.wait_ge(S["w_copied"], c)
                mm = each(lambda t, h, u: mul(cell(4, t, h), head(m_k, h, u, slice(0, CHUNK)), head(v_tok, h, u),
                                              t == 0, not c and t == HT - 1))
                if c:
                    pe.wait_ge(S["state"], c)
                    mm = each(lambda t, h, u: mul(cell(4, t, h), decayed(0, u, h), head(state_t, h, t), False,
                                                  t == HT - 1))
                mm.then_inc(S["w_summed"], told.one("w_summed"))
                if c > 0:
                    pe.wait_ge(S["y_copied"], c)
                each(lambda t, h, u: mul(cell(7, t, h), head(v_tok, h, u), head(m_k, h, u, slice(CHUNK, P)),
                                         t == 0, False))
                if c:
                    each(lambda t, h, u: mul(cell(7, t, h), head(state_t, h, t), decayed(1, u, h), False, False))
                pe.wait_ge(S["w_copied"], c + 1)
                if c > 0:
                    pe.wait_ge(S["sa_copied"], c)
                each(lambda t, h, u: mul(cell(5, t, h), head(xt_inv, h, u), head(w_s, h, t), True, True)).then_inc(
                    S["sa_summed"], told.one("sa_summed"))
                if c < NCH - 1:
                    each(lambda t, h, u: mul(cell(6, t, h), head(k_tok, h, u), head(v_tok, h, u), t == 0, False))
                    pe.wait_ge(S["sa_copied"], c + 1)
                    each(lambda t, h, u: mul(cell(6, t, h), head(b_tok, h, u), head(sa_s, h, t), False,
                                             t == HT - 1)).then_inc(S["state_summed"], told.one("state_summed"))
                pe.wait_ge(S["sa_copied"], c + 1)
                each(lambda t, h, u: mul(cell(7, t, h), head(sa_s, h, t), head(m_b, h, u, slice(CHUNK, P)),
                                         False, t == HT - 1)).then_inc(S["y_summed"], told.one("y_summed"))
            pe.wait_ge(S["y_copied"], NCH)
            for t in range(HT):
                mm = pe.matmul(bank[4 + t // 2][:, t % 2 * T:t % 2 * T + T], head_ones[:, :], y_t[:, t, :],
                               start=True, stop=True)
            mm.then_inc(S["y_mean"], told.one("y_mean"))
            pe.wait_ge(S["forget_read"], 1)
            for k in range(3):
                pe.wait_ge(S["late_squared"], k + 1)
                head_sums(late_sq)
                columns(B_GA + k)
                pe.wait_ge(S["factors"], k + 2)
                if 2 * k > 0:
                    pe.wait_ge(S["normed_by_head"], 2 * k)
                if k == 2:
                    pe.wait_ge(S["y_centred"], 2)
                turn_factors(late, 4 if k == 2 else 6)
            for it in range(FUNITS + 1):
                if it < FUNITS:
                    t, i = divmod(it, TT)
                    w = P * (i + 1)
                    pe.wait_ge(S["normed_by_head"], 6)
                    if 2 * it > 0:
                        pe.wait_ge(S["f_scores_read"], 2 * it)
                    for h in range(2):
                        o = bank[4 + h][:, 0:w]
                        c = 32 + 2 * t + h
                        pe.matmul(o, head(fq, h, t, slice(i * P, (i + 1) * P)), head(fk, h, t, slice(0, w)),
                                  start=True, stop=False)
                        mm = pe.matmul(o, ident[32:32 + NH, c:c + 1].to_broadcast([NH, P]), forget[32:32 + NH, 0:w],
                                       start=False, stop=True)
                    mm.then_inc(S["f_scores"], told.one("f_scores"))
                if it < 5:
                    columns(B_GA + 3 + it)
                elif it < 7:
                    r = it - 5
                    pe.wait_ge(S["y_lo"], 1)
                    for b, c in enumerate(all_read(B_RP)):
                        pe.wait_ge(S[f"bank{b}_read"], c)
                    by_rows(B_RP + r, (B_RP + r) % RING, 0, Y_hi, Y_lo, 2 * r, r == 0, r == 1)
                if it:
                    t, i = divmod(it - 1, TT)
                    pe.wait_ge(S["f_probs"], it)
                    if it - 1 > 0:
                        pe.wait_ge(S["fpT_ready"], it - 1)
                    w = P * (i + 1)
                    for b in range(2 * (i + 1)):
                        mm = pe.transpose(bank[6][:, b * P:(b + 1) * P], fs_t[:, (it - 1) % 2, b * P:(b + 1) * P],
                                          ident[:])
                    mm.then_inc(S["f_probs_turned"], told.one("f_probs_turned"))
                if it:
                    pe.wait_ge(S["fpT_ready"], it)
                    if it - 1 > 0:
                        pe.wait_ge(S["f_out_lo"], it - 1)
                    for h in range(2):
                        for kb in range(i + 1):
                            b = h * (i + 1) + kb
                            c = (2 * t + h) * HD
                            mm = pe.matmul(head(bank[7], h, slice(0, P)), fv[:, kb, c:c + HD],
                                           fpT[:, b * P:(b + 1) * P], start=kb == 0, stop=kb == i)
                    mm.then_inc(S["f_pv_done"], told.one("f_pv_done"))
            for n in range(B_FP, ffn_at[2]):
                if n < B_WO:
                    r = n - B_FP
                    pe.wait_ge(S["f_out_lo"], FUNITS)
                    by_rows(n, n % RING, 4, Y_hi, Y_lo, HT + 2 * r, r == 0, r == 1)
                else:
                    r = n - B_WO
                    pe.wait_ge(S["mixed_lo"], 4 + r + 1)
                    by_rows(n, n % RING, 0, X_hi, X_lo, 2 * r, r == 0, r == 3, final=r == 3)

        def act_mixer(told, act, a, split, square, root, spread, state):
            def copies(ready, count, dst, b, name):
                act.wait_ge(S[ready], count)
                for f in range(2):
                    done = name
                    a.activation(flat(dst[:, 8 * f:8 * f + 8, :]), bank[b + f][:, :], ACT.Copy).then_inc(
                        S[done], told.one(done))

            act.wait_ge(S["lora_shifted"], 1)
            a.activation(lora_act[0:32, 0, :], lora_act[0:32, 0, :], ACT.Tanh).then_inc(
                S["lora_act"], told.one("lora_act"))
            a.activation(lora_act[64:128, 0, :], lora_act[64:128, 0, :], ACT.Sigmoid).then_inc(
                S["lora_act"], told.one("lora_act"))
            a.activation(lora_act[0:32, 1, :], lora_act[0:32, 1, :], ACT.Sigmoid).then_inc(
                S["lora_act"], told.one("lora_act"))
            split(B0 + 3)
            for ready, b, dst, gain, name in (("decay_in", 6, dec, "rwkv_w0_2", "decay_read"),
                                              ("rate_in", 4, rate, "rwkv_a0_2", "rate_read")):
                act.wait_ge(S[ready], 1)
                for t in range(HT):
                    done = name or "act_step"
                    a.activation(dst[:, t, :], bank[b + t // 2][:, t % 2 * T:t % 2 * T + T], ACT.Sigmoid,
                                 bias=col(gain, t)).then_inc(S[done], told.one(done))
            split(B0 + 4)
            act.wait_ge(S["kk_raw"], HT)
            a.activation(flat(early), flat(kk), ACT.Square).then_inc(S["kk_squared"], told.one("kk_squared"))
            split(B0 + 5)
            act.wait_ge(S["head_sums"], 1)
            a.activation(head_col, bank[3][:, 256:272], ACT.Sqrt, bias=eps[:, 3:4], scale=1.0).then_inc(
                S["head_root"], told.one("head_root"))
            split(B0 + 6)
            act.wait_ge(S["gate_in"], 1)
            for f in range(2):
                a.activation(flat(g_out[:, 2 * f:2 * f + 2, :]), bank[6 + f][:, :], ACT.Copy).then_inc(
                    S["g_read"], told.one("g_read"))
            act.wait_ge(S["forget_abs"], 1)
            z = lora_in[32:32 + NH, 0, 1:T + 1]
            a.activation(z, z, ACT.Exp).then_inc(S["act_step"], told.one("act_step"))
            act.wait_ge(S["act_step"], told.value("act_step"))
            a.activation(z, z, ACT.Ln, bias=ones[32:32 + NH, 0:1], scale=1.0).then_inc(
                S["forget_log"], told.one("forget_log"))
            split(B0 + 7)
            act.wait_ge(S["sums"], 1)
            a.activation(flat(dec_prev), flat(dec_prev), ACT.Exp).then_inc(S["decays"], told.one("decays"))
            a.activation(flat(dec), flat(dec_inv), ACT.Exp).then_inc(S["decays"], told.one("decays"))
            a.activation(flat(dec_inv), flat(dec_inv), ACT.Exp, scale=-1.0).then_inc(S["decays"], told.one("decays"))
            for n in range(B_FOX + 1, B_FOX + 4):
                split(n)
            copies("b_turned", 1, b_tok, 6, "b_tok")
            copies("k_turned", 1, k_tok, 4, "k_tok")
            copies("v_turned", 1, v_tok, 6, "v_tok")
            copies("x_first", 1, x_inv, 4, "x_copied")
            for n in range(1, LEVELS + 1):
                for f in range(2):
                    if f and n > 1:
                        split(B_FOX + n + 2)
                    act.wait_ge(S["p1"], 2 * (n - 1) + f + 1)
                    a.activation(half_1[:, f, :], bank[4 + f][:, :], ACT.Copy).then_inc(
                        S["p1_copied"], told.one("p1_copied"))
                if n >= 4:
                    m = B_FOX + n
                    act.wait_ge(S["chunk_used"], m + 1)
                    v = [a.activation(fv[:, t, 256 * (n - 4):256 * (n - 3)], bank[bank_of[m]][:, t * T:t * T + T],
                                      ACT.Copy, scale=rcol[:, t:t + 1]) for t in range(TT)]
                    v[0].then_inc(S["v_half"], 1)
                    v[1].then_inc(S[f"bank{bank_of[m]}_read"], 1)
            for c in range(NCH):
                act.wait_ge(S["w_summed"], c + 1)
                a.activation(flat(w_s), bank[4][:, 0:T], ACT.Copy).then_inc(S["w_copied"], told.one("w_copied"))
                act.wait_ge(S["sa_summed"], c + 1)
                a.activation(flat(sa_s), bank[5][:, 0:T], ACT.Copy).then_inc(S["sa_copied"], told.one("sa_copied"))
                act.wait_ge(S["y_summed"], c + 1)
                a.activation(y_t[:, :, c * CHUNK:(c + 1) * CHUNK],
                             bank[7][:, 0:T].rearrange("p (t s) -> p t s", t=HT), ACT.Copy).then_inc(
                    S["y_copied"], told.one("y_copied"))
            for k, (src, e) in enumerate(((fq, 0), (fk, 0), (y_t, 2))):
                act.wait_ge(S["head_sums"], k + 1)
                if k == 2:
                    act.wait_ge(S["y_centred"], 2)
                if k == 0:
                    for m in range(B_FOX, B_FOX + 4):
                        act.wait_ge(S[f"bank{bank_of[m]}_read"], reads[m])
                a.activation(flat(late_sq), flat(src), ACT.Square).then_inc(S["late_squared"], told.one("late_squared"))
                act.wait_ge(S["head_sums"], k + 2)
                a.activation(head_col, bank[3][:, 256:272], ACT.Sqrt, bias=eps[:, e:e + 1], scale=1.0 / HD).then_inc(
                    S["head_root"], told.one("head_root"))
                split(B_GA + k + 2)
            for it in range(FUNITS + 1):
                if it < FUNITS:
                    w = P * (it % TT + 1)
                    act.wait_ge(S["f_row_max"], it + 1)
                    for h in range(2):
                        a.activation(fs_t[:, it % 2, h * w:h * w + w], fs_t[:, it % 2, h * w:h * w + w], ACT.Exp,
                                     bias=nmax[:, it % 2, h:h + 1], accum_out=den[:, it % 2, h:h + 1]).then_inc(
                            S["f_exp"], told.one("f_exp"))
                        act.wait_ge(S["f_exp"], told.value("f_exp"))
                if it < 7:
                    split(B_GA + 3 + it + 2)
                if it:
                    w = 2 * P * ((it - 1) % TT + 1)
                    act.wait_ge(S["f_probs_turned"], it)
                    a.activation(fpT[:, 0:w], bank[6][:, 0:w], ACT.Copy).then_inc(S["fpT_ready"], told.one("fpT_ready"))
                if it == 2:
                    act.wait_ge(S["y_ready"], 1)
                    a.activation(Y_hi[:, 0:HT, :], y_t, ACT.Copy).then_inc(S["y_hi"], told.one("y_hi"))
                if it:
                    t, i = divmod(it - 1, TT)
                    act.wait_ge(S["f_pv_done"], it)
                    a.activation(Y_hi[:, HT + t, i * P:(i + 1) * P], bank[7][:, 0:P], ACT.Copy).then_inc(
                        S["f_out_hi"], told.one("f_out_hi"))
            for n in range(B_FP, ffn_at[2]):
                split(n + 2)
                if n == B_FP:
                    for g, lo in ((gate_2a, 0), (gate_2b, 4)):
                        for m in range(B_GA + lo, B_GA + lo + 4):
                            act.wait_ge(S[f"bank{bank_of[m]}_read"], reads[m])
                        a.activation(flat(g), flat(g), ACT.Sigmoid).then_inc(S["gate_2"], told.one("gate_2"))
                for p in ((0, 1) if n == B_WO - 1 else (2, 3) if n == B_WO else ()):
                    act.wait_ge(S["mixed"], 4 + p + 1)
                    a.activation(X_hi[:, 2 * p:2 * p + 2, :], gate_2a[:, 2 * p:2 * p + 2, :], ACT.Copy).then_inc(
                        S["mixed_hi"], told.one("mixed_hi"))

        def dve_mixer(told, dve, v, split, diagonals, out_bank, state):
            v.memset(unshifted[:, :, 0:1], 0.0).then_inc(S["dve_step"], told.one("dve_step"))
            dve.wait_ge(S["dve_step"], told.value("dve_step"))
            v.memset(lora_in[:, :, 0:1], 0.0).then_inc(S["dve_step"], told.one("dve_step"))
            dve.wait_ge(S["dve_step"], told.value("dve_step"))
            v.tensor_scalar(q_gain, col("fox_q_norm_2"), HD ** -0.5, None, ALU.mult).then_inc(
                S["dve_step"], told.one("dve_step"))
            v.tensor_scalar(kept, par[:, rows["rwkv_k_a_2"]:rows["rwkv_k_a_2"] + HT], -1.0, 1.0, ALU.mult,
                            ALU.add).then_inc(S["dve_step"], told.one("dve_step"))
            dve.wait_ge(S["dve_step"], told.value("dve_step"))

            def shifted_columns(n):
                j = KRV[n - B0 - 1]
                split(n + 2)
                u, dst = unshifted[:, n % 2 * 2:n % 2 * 2 + 2, :], (r_s, k_s, v_s)[j // 2][:, j % 2 * 2:j % 2 * 2 + 2, :]
                out_bank(n, u[:, :, 1:T + 1])
                v.tensor_tensor(dst, u[:, :, 0:T], u[:, :, 1:T + 1], ALU.subtract).then_inc(
                    S["dve_step"], told.one("dve_step"))
                dve.wait_ge(S["dve_step"], told.value("dve_step"))
                for m in range(2):
                    v.scalar_tensor_tensor(out=dst[:, m, :], in0=dst[:, m, :], scalar=col("mu", 2 * j + m),
                                           in1=u[:, m, 1:T + 1], op0=ALU.mult, op1=ALU.add).then_inc(
                        S["shifted"], told.one("shifted"))
                dve.wait_ge(S["shifted"], told.value("shifted"))

            split(B0 + 2)
            out_bank(B0, lora_in[:, :, 1:T + 1])
            v.tensor_tensor(early[:, 0:2, :], lora_in[:, :, 0:T], lora_in[:, :, 1:T + 1], ALU.subtract).then_inc(
                S["dve_step"], told.one("dve_step"))
            dve.wait_ge(S["dve_step"], told.value("dve_step"))
            v.scalar_tensor_tensor(out=lora_act[:, 0, :], in0=early[:, 0, :], scalar=col("mu", 12),
                                   in1=lora_in[:, 0, 1:T + 1], op0=ALU.mult, op1=ALU.add).then_inc(
                S["dve_step"], told.one("dve_step"))
            dve.wait_ge(S["dve_step"], told.value("dve_step"))
            v.scalar_tensor_tensor(out=lora_act[0:32, 1, :], in0=early[0:32, 1, :],
                                   scalar=col("mu_tail", 0, 0, 32), in1=lora_in[0:32, 1, 1:T + 1],
                                   op0=ALU.mult, op1=ALU.add).then_inc(S["lora_shifted"], told.one("lora_shifted"))
            dve.wait_ge(S["lora_shifted"], told.value("lora_shifted"))
            rows_f = slice(32, 32 + NH)
            z, nabs = lora_in[rows_f, 1, 1:T + 1], lora_in[rows_f, 0, 1:T + 1]
            v.tensor_scalar(z, z, col("fox_f_bias_2", 0, 32, 32 + NH), None, ALU.add).then_inc(
                S["dve_step"], told.one("dve_step"))
            dve.wait_ge(S["dve_step"], told.value("dve_step"))
            v.tensor_scalar(nabs, z, -1.0, None, ALU.mult).then_inc(S["dve_step"], told.one("dve_step"))
            dve.wait_ge(S["dve_step"], told.value("dve_step"))
            v.tensor_tensor(nabs, nabs, z, ALU.min).then_inc(S["forget_abs"], told.one("forget_abs"))
            dve.wait_ge(S["forget_abs"], told.value("forget_abs"))
            shifted_columns(B0 + 1)
            shifted_columns(B0 + 2)
            for t in range(HT):
                v.tensor_scalar(kk[:, t, :], k_s[:, t, :], col("rwkv_k_k_2", t), None, ALU.mult).then_inc(
                    S["kk_raw"], told.one("kk_raw"))
            dve.wait_ge(S["decay_read"], HT)
            v.tensor_scalar(flat(dec), flat(dec), -EXP_HALF, None, ALU.mult).then_inc(
                S["dve_step"], told.one("dve_step"))
            dve.wait_ge(S["dve_step"], told.value("dve_step"))
            for t in range(HT):
                v.tensor_tensor_scan(dec_inv[:, t, :], resets[:], dec[:, t, :], 0.0, ALU.mult, ALU.add).then_inc(
                    S["dve_step"], told.one("dve_step"))
                dve.wait_ge(S["dve_step"], told.value("dve_step"))
            v.tensor_tensor(flat(dec_prev), flat(dec_inv), flat(dec), ALU.subtract).then_inc(
                S["sums"], told.one("sums"))
            dve.wait_ge(S["sums"], told.value("sums"))

            def factors(least, dst, count):
                dve.wait_ge(S["head_root"], count)
                if least:
                    v.tensor_scalar(head_col, head_col, least, None, ALU.max).then_inc(
                        S["dve_step"], told.one("dve_step"))
                    dve.wait_ge(S["dve_step"], told.value("dve_step"))
                v.reciprocal(head_col, head_col).then_inc(S["dve_step"], told.one("dve_step"))
                dve.wait_ge(S["dve_step"], told.value("dve_step"))
                v.tensor_copy(flat(dst).rearrange("p (h d) -> p h d", d=HD),
                              head_col[:, :, None].to_broadcast([P, 16, HD])).then_inc(
                    S["factors"], told.one("factors"))
                dve.wait_ge(S["factors"], told.value("factors"))

            shifted_columns(B0 + 3)
            factors(1e-12, early, 1)
            shifted_columns(B0 + 4)
            dve.wait_ge(S["forget_log"], 1)
            v.tensor_scalar(z, z, 0.0, None, ALU.min).then_inc(S["dve_step"], told.one("dve_step"))
            dve.wait_ge(S["dve_step"], told.value("dve_step"))
            v.tensor_tensor(nabs, nabs, z, ALU.subtract).then_inc(S["dve_step"], told.one("dve_step"))
            dve.wait_ge(S["dve_step"], told.value("dve_step"))
            v.tensor_tensor_scan(forget[rows_f, :], ones[rows_f, 0:1].to_broadcast([NH, T]), nabs, 0.0, ALU.mult,
                                 ALU.add).then_inc(S["forget"], told.one("forget"))
            dve.wait_ge(S["forget"], told.value("forget"))
            dve.wait_ge(S["factors_turned"], 1)
            for f in range(2):
                o = flat(kk[:, 2 * f:2 * f + 2, :])
                v.tensor_tensor(o, o, bank[4 + f][:, :], ALU.mult).then_inc(S["dve_step"], told.one("dve_step"))
                dve.wait_ge(S["dve_step"], told.value("dve_step"))
            dve.wait_ge(S["rate_read"], HT)
            for t in range(HT):
                v.tensor_scalar(early[:, t, :], rate[:, t, :], col("rwkv_k_a_2", t), kept[:, t:t + 1], ALU.mult,
                                ALU.add).then_inc(S["dve_step"], told.one("dve_step"))
                dve.wait_ge(S["dve_step"], told.value("dve_step"))
            v.tensor_tensor(flat(k_s), flat(k_s), flat(early), ALU.mult).then_inc(S["dve_step"], told.one("dve_step"))
            dve.wait_ge(S["dve_step"], told.value("dve_step"))
            v.tensor_tensor(flat(rate), flat(rate), flat(kk), ALU.mult).then_inc(S["dve_step"], told.one("dve_step"))
            dve.wait_ge(S["dve_step"], told.value("dve_step"))
            shifted_columns(B0 + 5)
            for t in range(HT):
                done = "rk_ready" if t == HT - 1 else "dve_step"
                v.scalar_tensor_tensor(out=early[:, t, :], in0=r_s[:, t, :], scalar=col("rwkv_r_k_2", t),
                                       in1=k_s[:, t, :], op0=ALU.mult, op1=ALU.mult).then_inc(S[done], told.one(done))
                dve.wait_ge(S[done], told.value(done))
            shifted_columns(B0 + 6)
            dve.wait_ge(S["forget_turned"], 1)
            v.tensor_copy(small[:, 8:24], bank[3][:, 256:272]).then_inc(S["forget_read"], told.one("forget_read"))
            dve.wait_ge(S["forget_read"], told.value("forget_read"))
            split(B_FOX + 2)
            out_bank(B_FOX, fq[:, 0:2, :])
            dve.wait_ge(S["bonus_in"], 1)
            for f in range(2):
                v.tensor_tensor(flat(bonus[:, 2 * f:2 * f + 2, :]), bank[6 + f][:, :],
                                flat(v_s[:, 2 * f:2 * f + 2, :]), ALU.mult).then_inc(
                    S["dve_step"], told.one("dve_step"))
                dve.wait_ge(S["dve_step"], told.value("dve_step"))
            dve.wait_ge(S["decays"], 3)
            v.tensor_tensor(flat(b_dec), flat(rate), flat(dec_inv), ALU.mult).then_inc(
                S["dve_step"], told.one("dve_step"))
            dve.wait_ge(S["dve_step"], told.value("dve_step"))
            v.tensor_tensor(flat(k_dec), flat(k_s), flat(dec_inv), ALU.mult).then_inc(
                S["dve_step"], told.one("dve_step"))
            dve.wait_ge(S["dve_step"], told.value("dve_step"))
            for t in range(HT):
                v.tensor_tensor(ar_part(1)[:, t], by_chunk(r_s)[:, t], by_chunk(dec)[:, t], ALU.mult).then_inc(
                    S["dve_step"], told.one("dve_step"))
                v.scalar_tensor_tensor(out=ar_part(0)[:, t], in0=by_chunk(kk)[:, t], scalar=-1.0,
                                       in1=by_chunk(dec_prev)[:, t], op0=ALU.mult, op1=ALU.mult).then_inc(
                    S["dve_step"], told.one("dve_step"))
                dve.wait_ge(S["dve_step"], told.value("dve_step"))
            v.tensor_copy(dec_end, dec[:, :, CHUNK - 1:T:CHUNK]).then_inc(S["decayed"], told.one("decayed"))
            dve.wait_ge(S["decayed"], told.value("decayed"))
            split(B_FOX + 3)
            out_bank(B_FOX + 1, fq[:, 2:4, :])
            dve.wait_ge(S["masks_ready"], 1)
            for c in range(NCH):
                for k, (dst, b) in enumerate(((m_b, 4), (m_k, 5))):
                    dve.wait_ge(S["chunk_scores"], 2 * c + k + 1)
                    v.tensor_tensor(dst[:, HT * c:HT * (c + 1), :],
                                    bank[b][:, :].rearrange("p (t s) -> p t s", t=HT), over(mask_2[:], HT),
                                    ALU.mult).then_inc(S["masked"], told.one("masked"))
                    dve.wait_ge(S["masked"], told.value("masked"))
            dve.wait_ge(S["k_turned"], 1)
            v.tensor_tensor(xt_inv, m_b[:, :, 0:CHUNK], over(levels[:, 0, :], NCH * HT), ALU.mult).then_inc(
                S["dve_step"], told.one("dve_step"))
            dve.wait_ge(S["dve_step"], told.value("dve_step"))
            v.tensor_tensor(xt_inv, xt_inv, over(eye[:], NCH * HT), ALU.add).then_inc(
                S["xt_first"], told.one("xt_first"))
            dve.wait_ge(S["xt_first"], told.value("xt_first"))
            for n in range(1, LEVELS + 1):
                for f in range(2):
                    v.tensor_tensor(half_n[:, f, :].rearrange("p (u s) -> p u s", u=8),
                                    m_b[:, 8 * f:8 * f + 8, 0:CHUNK], over(levels[:, n, :], 8), ALU.mult).then_inc(
                        S["off_ready"], told.one("off_ready"))
                    dve.wait_ge(S["off_ready"], told.value("off_ready"))
                for f in range(2):
                    if f and n > 1:
                        split(B_FOX + n + 2)
                    dve.wait_ge(S["p2"], 2 * (n - 1) + f + 1)
                    for b, dst in ((6, x_inv), (7, xt_inv)):
                        if b == 7 or n < LEVELS:
                            o = flat(dst[:, 8 * f:8 * f + 8, :])
                            done = "xt_added" if b == 7 else "dve_step"
                            v.tensor_tensor(o, o, bank[b][:, :], ALU.add).then_inc(S[done], told.one(done))
                            dve.wait_ge(S[done], told.value(done))
                    if f and 1 < n < 4:
                        out_bank(B_FOX + n, fk[:, 2 * (n % 2):2 * (n % 2) + 2, :])
            for c in range(NCH - 1):
                dve.wait_ge(S["state_summed"], c + 1)
                src = bank[6][:, 0:T].rearrange("p (t s) -> p t s", t=HT)
                if c:
                    v.tensor_tensor(state_t, state_t, src, ALU.add).then_inc(S["dve_step"], told.one("dve_step"))
                    dve.wait_ge(S["dve_step"], told.value("dve_step"))
                v.tensor_tensor(state_t, state_t if c else src,
                                dec_end[:, :, c:c + 1].to_broadcast([P, HT, CHUNK]), ALU.mult).then_inc(
                    S["state"], told.one("state"))
                dve.wait_ge(S["state"], told.value("state"))
            dve.wait_ge(S["y_mean"], 1)
            for f in range(2):
                o = flat(y_t[:, 2 * f:2 * f + 2, :])
                v.scalar_tensor_tensor(out=o, in0=bank[4 + f][:, :], scalar=-1.0 / HD, in1=o, op0=ALU.mult,
                                       op1=ALU.add).then_inc(S["y_centred"], told.one("y_centred"))
                dve.wait_ge(S["y_centred"], told.value("y_centred"))

            def gates(j):
                split(B_GA + j + 2)
                out_bank(B_GA + j, (gate_2a if j < 4 else gate_2b)[:, 2 * (j % 4):2 * (j % 4) + 2, :])

            for k in range(3):
                factors(None, late, k + 2)
                gates(k)
                dve.wait_ge(S["factors_turned"], k + 2)
                for t in range(HT):
                    o = bank[(4 if k == 2 else 6) + t // 2][:, t % 2 * T:t % 2 * T + T]
                    name = "normed_by_head" if t % 2 else None
                    if k == 2:
                        done = name or "dve_step"
                        v.tensor_tensor(y_t[:, t, :], y_t[:, t, :], o, ALU.mult).then_inc(S[done], told.one(done))
                        dve.wait_ge(S[done], told.value(done))
                    else:
                        q = (fq, fk)[k][:, t, :]
                        done = name or "dve_step"
                        v.scalar_tensor_tensor(out=q, in0=o, scalar=q_gain if k == 0 else col("fox_k_norm_2"),
                                               in1=q, op0=ALU.mult, op1=ALU.mult).then_inc(S[done], told.one(done))
                        dve.wait_ge(S[done], told.value(done))
            for it in range(FUNITS + 1):
                if it < FUNITS:
                    t, i = divmod(it, TT)
                    w = P * (i + 1)
                    dve.wait_ge(S["f_scores"], it + 1)
                    if it - 1 > 0:
                        dve.wait_ge(S["f_probs_turned"], it - 1)
                    for h in range(2):
                        v.scalar_tensor_tensor(out=fs_t[:, it % 2, h * w:h * w + w],
                                               in0=bank[4 + h][:, 0:w],
                                               scalar=forget_col[:, i, 2 * t + h:2 * t + h + 1],
                                               in1=causal[:, T - w:T], op0=ALU.subtract, op1=ALU.add).then_inc(
                            S["f_scores_read"], told.one("f_scores_read"))
                        dve.wait_ge(S["f_scores_read"], told.value("f_scores_read"))
                    v.tensor_reduce(nmax[:, it % 2, :], fs_t[:, it % 2, 0:2 * w].rearrange("p (h s) -> p h s", h=2),
                                    AX.X, ALU.max, negate=True).then_inc(S["f_row_max"], told.one("f_row_max"))
                    dve.wait_ge(S["f_row_max"], told.value("f_row_max"))
                if it:
                    b, w = (it - 1) % 2, P * ((it - 1) % TT + 1)
                    dve.wait_ge(S["f_exp"], 2 * it)
                    v.reciprocal(rden, den[:, b, :]).then_inc(S["dve_step"], told.one("dve_step"))
                    dve.wait_ge(S["dve_step"], told.value("dve_step"))
                    o = fs_t[:, b, 0:2 * w].rearrange("p (h s) -> p h s", h=2)
                    v.tensor_tensor(o, o, rden[:, :, None].to_broadcast([P, 2, w]), ALU.mult).then_inc(
                        S["f_probs"], told.one("f_probs"))
                    dve.wait_ge(S["f_probs"], told.value("f_probs"))
                if it < 5:
                    gates(3 + it)
                elif it < 7:
                    split(B_GA + 3 + it + 2)
                if it == 1:
                    for t in range(HT):
                        v.tensor_scalar(y_t[:, t, :], y_t[:, t, :], col("rwkv_lnx_g_2", t),
                                        col("rwkv_lnx_b_2", t), ALU.mult, ALU.add).then_inc(
                            S["dve_step"], told.one("dve_step"))
                        dve.wait_ge(S["dve_step"], told.value("dve_step"))
                    v.tensor_tensor(flat(y_t), flat(y_t), flat(bonus), ALU.add).then_inc(
                        S["dve_step"], told.one("dve_step"))
                    dve.wait_ge(S["dve_step"], told.value("dve_step"))
                    v.tensor_tensor(flat(y_t), flat(y_t), flat(g_out), ALU.mult).then_inc(
                        S["y_ready"], told.one("y_ready"))
                    dve.wait_ge(S["y_ready"], told.value("y_ready"))
                if it == 3:
                    dve.wait_ge(S["y_hi"], 1)
                    v.tensor_tensor(Y_lo[:, 0:HT, :], y_t, Y_hi[:, 0:HT, :].bitcast(F32), ALU.subtract).then_inc(
                        S["y_lo"], told.one("y_lo"))
                    dve.wait_ge(S["y_lo"], told.value("y_lo"))
                if it:
                    t, i = divmod(it - 1, TT)
                    dve.wait_ge(S["f_out_hi"], it)
                    v.tensor_tensor(Y_lo[:, HT + t, i * P:(i + 1) * P], bank[7][:, 0:P],
                                    Y_hi[:, HT + t, i * P:(i + 1) * P].bitcast(F32), ALU.subtract).then_inc(
                        S["f_out_lo"], told.one("f_out_lo"))
                    dve.wait_ge(S["f_out_lo"], told.value("f_out_lo"))
            for n in range(B_FP, ffn_at[2]):
                split(n + 2)
                if n == B_FP:
                    dve.wait_ge(S["gate_2"], 1)
                    dve.wait_ge(S["chunk_used"], B_FP)
                    for p in range(4):
                        o = gate_2a[:, 2 * p:2 * p + 2, :]
                        v.tensor_tensor(o, o, pairs(p), ALU.mult).then_inc(S["dve_step"], told.one("dve_step"))
                        dve.wait_ge(S["dve_step"], told.value("dve_step"))
                ps = (0, 1) if n == B_WO - 1 else (2, 3) if n == B_WO else ()
                for p in ps:
                    dve.wait_ge(S["gate_2"], 2)
                    dve.wait_ge(S["chunk_used"], B_WO)
                    ga, gb = gate_2a[:, 2 * p:2 * p + 2, :], gate_2b[:, 2 * p:2 * p + 2, :]
                    v.tensor_tensor(gb, gb, pairs(4 + p), ALU.mult).then_inc(S["dve_step"], told.one("dve_step"))
                    dve.wait_ge(S["dve_step"], told.value("dve_step"))
                    v.tensor_tensor(ga, ga, gb, ALU.add).then_inc(S["mixed"], told.one("mixed"))
                for p in ps:
                    ga = gate_2a[:, 2 * p:2 * p + 2, :]
                    dve.wait_ge(S["mixed_hi"], 4 + p + 1)
                    v.tensor_tensor(X_lo[:, 2 * p:2 * p + 2, :], ga, X_hi[:, 2 * p:2 * p + 2, :].bitcast(F32),
                                    ALU.subtract).then_inc(S["mixed_lo"], told.one("mixed_lo"))

        block = ctx.enter_context(nc.Block())

        @block.sync
        def _(sp):
            told = Count()

            def load(n, slot, parts):
                if not isinstance(n, int) or n >= RING:
                    sp.wait_ge(S["w_lo_dve"], n - 2)
                    sp.wait_ge(S["w_lo_pool"], n - 2)
                for src, c0 in parts:
                    k, c = src.shape[1], src.shape[2]
                    dst = raw[slot][:, :].rearrange("p (k c) -> p k c", k=k)[:, :, c0:c0 + c]
                    sp.dma_start(dst, src).then_inc(S[f"w_landed{slot}"], 16)

            sp.dma_start(x_in, inp["x"].rearrange("a (t p) d -> p (a t) d", p=P)).then_inc(S["x_landed"], 16)
            n = 0
            while n < TOTAL:
                if n in ffn_at.values():
                    k = [k for k, b in ffn_at.items() if b == n][0]
                    load(n, n % RING, chunks[n])
                    load(n + 1, (n + 1) % RING, chunks[n + 1])

                    def body(i):
                        for u, src in enumerate((gate_source(k, i + 1), val_source(k, i + 1), down_source(k, i))):
                            load(n + 2 + u + 3 * i, (n + 2 + u) % RING, ((src, 0),))

                    with sp.Fori(0, FPAIRS - 2) as i:
                        body(i)
                    body(FPAIRS - 2)
                    n += 3 * FPAIRS - 1
                load(n, n % RING, chunks[n])
                n += 1
            for t in range(TT):
                for h in range(2):
                    sp.wait_ge(S["out_ready"], 2 * t + h + 1)
                    sp.dma_start(out[0, t * P:(t + 1) * P, 512 * h:512 * (h + 1)],
                                 out_t[:, t, 512 * h:512 * (h + 1)]).then_inc(S["out_stored"], 16)
            sp.wait_ge(S["out_stored"], 16 * 2 * TT)
        runs = bucket_runs()
        UNITS = HPG * TT
        SCALE = HEAD ** -0.5

        def tap(side, i, m, k):
            return par[:, bass.ds(i * 2 + (rows["ffn_conv_w"] + k * 2 * FT + side * FT + m), 1)]

        def tap_bias(side, i, m):
            return par[:, bass.ds(i * 2 + (rows["ffn_conv_b"] + side * FT + m), 1)]

        @block.gpsimd
        def _(pool):
            told = Count()
            g = nc.gpsimd

            def diagonal(v, base, pattern, name=None):
                done = name or "pool_step"
                g.affine_select(out=v, in_=v, compare_op=ALU.not_equal, fill=1.0, base=base,
                                pattern=pattern, channel_multiplier=1).then_inc(S[done], told.one(done))
                pool.wait_ge(S[done], told.value(done))

            g.memset(par_in, 0.0).then_inc(S["par_cleared"], told.one("par_cleared"))
            pool.wait_ge(S["par_cleared"], told.value("par_cleared"))
            g.memset(ident[:], 0.0).then_inc(S["pool_step"], told.one("pool_step"))
            pool.wait_ge(S["pool_step"], told.value("pool_step"))
            diagonal(ident[:], 0, [[-1, P]], "ident_ready")
            g.memset(eps[:, 0:1], 1e-6).then_inc(S["pool_step"], told.one("pool_step"))
            g.memset(eps[:, 1:2], 1e-5).then_inc(S["pool_step"], told.one("pool_step"))
            g.memset(eps[:, 2:3], 64e-5).then_inc(S["pool_step"], told.one("pool_step"))
            g.memset(eps[:, 3:4], 0.0).then_inc(S["pool_step"], told.one("pool_step"))
            g.memset(ones[:], 1.0).then_inc(S["pool_step"], told.one("pool_step"))
            pool.wait_ge(S["pool_step"], told.value("pool_step"))
            g.memset(onehot[0:BUCKETS, :], 0.0).then_inc(S["pool_step"], told.one("pool_step"))
            pool.wait_ge(S["pool_step"], told.value("pool_step"))
            g.memset(table[0:HPG], NEG).then_inc(S["pool_step"], told.one("pool_step"))
            pool.wait_ge(S["pool_step"], told.value("pool_step"))
            exact = BUCKETS // 2
            diagonal(onehot[0:BUCKETS, T - exact:T], 1 - exact, [[1, exact]])
            for b, near, far in runs:
                diagonal(onehot[0:BUCKETS, T - 1 - far:T - near], -b, [[0, far - near + 1]])
            g.memset(head_ones[:], 0.0).then_inc(S["pool_step"], told.one("pool_step"))
            pool.wait_ge(S["pool_step"], told.value("pool_step"))
            g.memset(head_ones[0:HD, 0:HD], 1.0).then_inc(S["pool_step"], told.one("pool_step"))
            pool.wait_ge(S["pool_step"], told.value("pool_step"))
            g.memset(head_ones[HD:P, HD:P], 1.0).then_inc(S["pool_step"], told.one("pool_step"))
            pool.wait_ge(S["pool_step"], told.value("pool_step"))
            g.memset(zeros_r[:].bitcast(F32), 0.0).then_inc(S["pool_step"], told.one("pool_step"))
            pool.wait_ge(S["pool_step"], told.value("pool_step"))
            g.memset(c_pad[:, :, 0:PAD], 0.0).then_inc(S["constants"], told.one("constants"))
            pool.wait_ge(S["constants"], told.value("constants"))

            def split(n, slot):
                pool.wait_ge(S["w_hi"], n + 1)
                g.tensor_tensor(w_lo[slot][:, LO_DVE:CW], raw[slot][:, LO_DVE:CW],
                                w_hi[slot][:, LO_DVE:CW].bitcast(F32), ALU.subtract).then_inc(
                    S["w_lo_pool"], told.one("w_lo_pool"))

            split(0, 0)
            split(1, 1)
            pool.wait_ge(S["table_ready"], GROUPS)
            pool.dma_start(scratch.rearrange("g h d -> h g d"), table[0:HPG]).then_inc(S["table_stored"], 16)
            pool.wait_ge(S["table_stored"], 16)
            src = bass.AP(scratch.tensor, scratch.offset + P - 1, [[384, GROUPS * HPG], [-1, P], [1, T]])
            pool.dma_start(shifted, src).then_inc(S["table_shifted"], 16)
            pool.wait_ge(S["table_shifted"], 16)
            pool.dma_start(bias_t, shifted.rearrange("h p c -> p h c")).then_inc(S["bias_landed"], 16)

            n = 2
            while n < TOTAL:
                if n == A_GA + 2:
                    second_constants(told, pool, g)
                if n == B0:
                    for row, part, ap in ((0, 0, inp["rwkv_w_up_2"]), (32, 0, inp["rwkv_a_up_2"]),
                                          (64, 0, inp["rwkv_g_up_2"][:, 0:HD, :]),
                                          (0, 1, inp["rwkv_g_up_2"][:, HD:96, :])):
                        k = ap.shape[1]
                        pool.dma_start(lora_w[row:row + k, part, :], ap[0]).then_inc(S["lora_landed"], 16)
                if n in ffn_at.values():
                    with pool.Fori(0, FPAIRS) as i:
                        told.enter(i, {"w_lo_pool": 3})
                        for u in range(3):
                            split(i * 3 + (n + u), (n + u) % RING)
                        told.leave(FPAIRS)
                    n += 3 * FPAIRS
                else:
                    split(n, n % RING)
                    n += 1

        @block.scalar
        def _(act):
            told = Count()
            a = nc.scalar
            state = {"norm": 0, "upd": 0, "spread": 0, "ffn": 0}

            def split(n, slot=None, land=None):
                if isinstance(n, int):
                    if n >= TOTAL:
                        return
                    slot, land = n % RING, landed[n]
                act.wait_ge(S[f"w_landed{slot}"], land)
                if due(n - 2):
                    act.wait_ge(S["chunk_used"], n - 2)
                a.activation(w_hi[slot][:, :], raw[slot][:, :], ACT.Copy).then_inc(S["w_hi"], told.one("w_hi"))

            def square(p, source):
                if 4 * state["norm"] + p - 3 > 0:
                    act.wait_ge(S["sq_used"], 4 * state["norm"] + p - 3)
                a.activation(sq[:, p, :], source, ACT.Square).then_inc(S["sq_ready"], told.one("sq_ready"))

            def root(e):
                a.activation(small[:, 61:62], ones[:, 0:1], ACT.Sqrt)
                act.wait_ge(S["sq_used"], 4 * state["norm"] + 4)
                a.activation(rcol[:, 2:4], bank[3][:, 256:258], ACT.Sqrt, bias=eps[:, e:e + 1],
                             scale=1.0 / D).then_inc(S["column"], told.one("column"))
                act.wait_ge(S["column"], told.value("column"))
                state["norm"] += 1

            def spread():
                state["spread"] += 1
                act.wait_ge(S["spread"], state["spread"])
                a.activation(rstd[:], bank[3][:, 0:T], ACT.Copy).then_inc(S["rstd"], told.one("rstd"))
                act.wait_ge(S["rstd"], told.value("rstd"))

            def x_scaled(gain, ahead):
                for p in range(4):
                    act.wait_ge(S["x_updated"], 4 * state["upd"] + p + 1)
                    for t in (2 * p, 2 * p + 1):
                        a.activation(X_hi[:, t, :], x[:, t, :], ACT.Copy, scale=col(gain, t)).then_inc(
                            S["xg_hi"], told.one("xg_hi"))
                    square(p, flat(x[:, 2 * p:2 * p + 2, :]))
                state["upd"] += 1
                root(0)
                split(ahead)
                spread()

            def post_norm(last):
                for p in range(4):
                    if p < 3:
                        act.wait_ge(S["pair_summed"], 3 * LAYER_ENDS.index(last) + p + 1)
                    else:
                        act.wait_ge(S["chunk_used"], last)
                    square(p, bank[4 + p][:, :])
                root(0)
                spread()

            act.wait_ge(S["par_cleared"], 1)
            for group, row, lo, ap in staged:
                n, c = ap.shape
                act.dma_start(par_in[row:row + n, group, lo:lo + c], ap).then_inc(S["par_landed"], 16)
            act.dma_start(heads[0:BUCKETS, 0:GROUPS * HPG], inp["rel_bias"]).then_inc(S["rel_landed"], 16)
            split(0)
            split(1)
            act.wait_ge(S["constants"], 1)
            act.wait_ge(S["par_ready"], 2)
            x_scaled("norm_mix_pre", 2)

            def feed(k):
                b0, before = ffn_at[k], FPAIRS * state["ffn"]
                state["ffn"] += 1

                def taps(side, i, name):
                    for m in range(2):
                        done = name or "act_step"
                        a.activation(acc[:, side, m, :], u_t[:, side, m * T:m * T + T], ACT.Identity,
                                     bias=tap_bias(side, i, m), scale=tap(side, i, m, 2)).then_inc(
                            S[done], told.one(done))

                def gate_part(i):
                    act.wait_ge(S["gate_read"], i + (before + 1))
                    if k == 0:
                        taps(0, i, "taps_gate")
                    else:
                        a.activation(act_t, u_t[:, 0], ACT.Silu).then_inc(S["act_gate"], told.one("act_gate"))
                        act.wait_ge(S["act_gate"], told.value("act_gate"))

                def val_part(i):
                    if k == 0:
                        act.wait_ge(S["val_read"], i + (before + 1))
                        taps(1, i, "taps_val")
                        act.wait_ge(S["conv_gate"], i + 1)
                        a.activation(act_t, flat(acc[:, 0]), ACT.Gelu_apprx_tanh).then_inc(
                            S["act_gate"], told.one("act_gate"))
                        act.wait_ge(S["act_gate"], told.value("act_gate"))
                    act.wait_ge(S["f_ready"], i + (before + 1))
                    act.wait_ge(S["chunk_used"], i * 3 + (b0 + 2))
                    a.activation(flat(Y_hi[:, 0:2, :]), f_t, ACT.Copy).then_inc(S["f_hi"], told.one("f_hi"))

                def body(i):
                    for u in range(3):
                        if u == 1:
                            val_part(i)
                        if u == 2:
                            gate_part(i + 1)
                        m = b0 + 4 + u
                        if isinstance(i, int):
                            split(m + 3 * i)
                        else:
                            split(i * 3 + m, m % RING, i * 16 + landed[m])

                gate_part(0)
                split(b0 + 3)
                with act.Fori(0, FPAIRS - 2) as i:
                    per = {"w_hi": 3, "f_hi": 1, "act_gate": 1}
                    if k == 0:
                        per.update({"taps_gate": 2, "taps_val": 2})
                    told.enter(i, per)
                    body(i)
                    told.leave(FPAIRS - 2)
                body(FPAIRS - 2)
                split(b0 + 34)
                val_part(FPAIRS - 1)

            for n in range(A_GA):
                if n:
                    split(n + 2)
                if n < A_QKV and n % 2 == 1:
                    act.wait_ge(S[f"bank{bank_of[n]}_read"], reads[n])
                    gate = glu[:, 1, n // 2 % 2, :]
                    a.activation(gate, gate, ACT.Sigmoid).then_inc(S["glu_sigmoid"], told.one("glu_sigmoid"))
                    act.wait_ge(S["glu_sigmoid"], told.value("glu_sigmoid"))
                if n >= A_QKV + 12:
                    j = n - A_QKV - 12
                    act.wait_ge(S["chunk_used"], n + 1)
                    v = [a.activation(v_t[:, t, 256 * j:256 * j + 256], bank[n % 3][:, 256 * t:256 * t + 256],
                                      ACT.Copy, scale=rcol[:, t:t + 1]) for t in range(TT)]
                    v[0].then_inc(S["v_half"], 1)
                    v[1].then_inc(S[f"bank{n % 3}_read"], 1)
            for it in range(UNITS + 1):
                if it < UNITS:
                    w = GROUPS * P * (it % TT + 1)
                    act.wait_ge(S["row_max"], it + 1)
                    a.activation(s_t[:, it % 2, 0:w], s_t[:, it % 2, 0:w], ACT.Exp,
                                 bias=small[:, it % 2:it % 2 + 1],
                                 accum_out=small[:, 2 + it % 2:3 + it % 2]).then_inc(
                        S["exp_done"], told.one("exp_done"))
                    act.wait_ge(S["exp_done"], told.value("exp_done"))
                if it < UNITS:
                    split(A_GA + it + 2)
                if it:
                    nb = GROUPS * ((it - 1) % TT + 1)
                    act.wait_ge(S["probs_turned"], it)
                    if nb > 4:
                        a.activation(pT[:, 512:nb * P], bank[7][:, 0:(nb - 4) * P], ACT.Copy).then_inc(
                            S["act_step"], told.one("act_step"))
                    k = min(nb, 4) * P
                    a.activation(pT[:, 0:k], bank[6][:, 0:k], ACT.Copy).then_inc(S["pT_ready"], told.one("pT_ready"))
                if it == 1:
                    act.wait_ge(S["mean_summed"], 1)
                    a.activation(rcol[:, 2:4], bank[3][:, 256:258], ACT.Copy, scale=1.0 / D).then_inc(
                        S["column"], told.one("column"))
                    act.wait_ge(S["column"], told.value("column"))
                    state["spread"] += 2
                if it == 3:
                    act.wait_ge(S["centred"], 1)
                    for p in range(4):
                        square(p, flat(conv[:, 2 * p:2 * p + 2, :]))
                    root(1)
                if it:
                    j, i = divmod(it - 1, TT)
                    act.wait_ge(S["pv_done"], it)
                    a.activation(Y_hi[:, j, i * P:(i + 1) * P], bank[3][:, 384:512], ACT.Copy).then_inc(
                        S["attn_hi"], told.one("attn_hi"))
            for n in range(A_AO, A_END):
                split(n + 2)
                if n == A_AO:
                    for t in range(2 * NT):
                        g, name = (gate_a, "gate_a") if t < NT else (gate_c, "gate_c")
                        act.wait_ge(S[f"bank{bank_of[A_GA + t // 2]}_read"], reads[A_GA + t // 2])
                        a.activation(g[:, t % NT, :], g[:, t % NT, :], ACT.Sigmoid,
                                     bias=col("b_gate", t)).then_inc(S[name], told.one(name))
                    act.wait_ge(S["normed"], 1)
                    for r in PW_ROWS:
                        for t in (2 * r, 2 * r + 1):
                            a.activation(conv[:, t, :], conv[:, t, :], ACT.Silu, bias=col("conv_ln_b", t),
                                         scale=col("conv_ln_g", t)).then_inc(S["silu"], told.one("silu"))
                    act.wait_ge(S["silu"], told.value("silu"))
                if n in (A_AO, A_AO + 1):
                    for r in PW_ROWS[:2] if n == A_AO else PW_ROWS[2:]:
                        if n > A_AO:
                            act.wait_ge(S["chunk_used"], A_PW)
                        a.activation(Y_hi[:, 2 * r:2 * r + 2, :], conv[:, 2 * r:2 * r + 2, :], ACT.Copy).then_inc(
                            S["silu_hi"], told.one("silu_hi"))
                if n >= A_WO - 1 and n < A_WO + 1:
                    for p in (0, 1) if n < A_WO else (2, 3):
                        act.wait_ge(S["mixed"], p + 1)
                        a.activation(X_hi[:, 2 * p:2 * p + 2, :], mixed_a[:, 2 * p:2 * p + 2, :], ACT.Copy).then_inc(
                            S["mixed_hi"], told.one("mixed_hi"))
            post_norm(A_END)
            x_scaled("norm_ffn_pre", ffn_at[0] + 2)
            feed(0)
            post_norm(ffn_at[1])
            x_scaled("ffn1_norm_2", ffn_at[1] + 2)
            feed(1)
            x_scaled("mix_norm_2", B0 + 2)
            act_mixer(told, act, a, split, square, root, spread, state)
            x_scaled("ffn2_norm_2", ffn_at[2] + 2)
            feed(2)
            for p in range(4):
                act.wait_ge(S["x_updated"], 4 * state["upd"] + p + 1)
                for t in (2 * p, 2 * p + 1):
                    a.activation(xg[:, t, :], x[:, t, :], ACT.Copy, scale=col("final_norm_2", t)).then_inc(
                        S["xf_ready"], told.one("xf_ready"))
                square(p, flat(x[:, 2 * p:2 * p + 2, :]))
            root(0)

        @block.vector
        def _(dve):
            told = Count()
            v = nc.vector
            state = {"column": 0, "rstd": 0, "xg": 0, "ffn": 0}

            def split(n, slot=None):
                if isinstance(n, int):
                    if n >= TOTAL:
                        return
                    slot = n % RING
                dve.wait_ge(S["w_hi"], n + 1)
                v.tensor_tensor(w_lo[slot][:, 0:LO_DVE], raw[slot][:, 0:LO_DVE],
                                w_hi[slot][:, 0:LO_DVE].bitcast(F32), ALU.subtract).then_inc(
                    S["w_lo_dve"], told.one("w_lo_dve"))

            def diagonals(invert=True):
                state["column"] += 1
                dve.wait_ge(S["column"], state["column"])
                c = 2
                if invert:
                    v.reciprocal(rcol[:, 0:2], rcol[:, 2:4]).then_inc(S["rcol"], told.one("rcol"))
                    dve.wait_ge(S["rcol"], told.value("rcol"))
                    c = 0
                v.tensor_scalar(diag[:, 0, :], ident[:], rcol[:, c:c + 1], None, ALU.mult).then_inc(
                    S["dve_step"], told.one("dve_step"))
                v.tensor_scalar(diag[:, 1, :], ident[:], rcol[:, c + 1:c + 2], None, ALU.mult).then_inc(
                    S["diagonals"], told.one("diagonals"))
                dve.wait_ge(S["diagonals"], told.value("diagonals"))

            def x_low(gain):
                for t in range(NT):
                    dve.wait_ge(S["xg_hi"], state["xg"] * NT + t + 1)
                    v.scalar_tensor_tensor(out=X_lo[:, t, :], in0=x[:, t, :], scalar=col(gain, t),
                                           in1=X_hi[:, t, :].bitcast(F32), op0=ALU.mult,
                                           op1=ALU.subtract).then_inc(S["xg_lo"], told.one("xg_lo"))
                state["xg"] += 1
                diagonals()
                state["rstd"] += 1

            def out_bank(n, dst, other=None):
                b = bank_of[n]
                dve.wait_ge(S["chunk_used"], n + 1)
                dve.wait_ge(S["rstd"], state["rstd"])
                v.tensor_tensor(dst, pairs(b), over(rstd[:], 2), ALU.mult).then_inc(S[f"bank{b}_read"], 1)
                dve.wait_ge(S[f"bank{b}_read"], reads[n])

            def post_norm(gain):
                diagonals()
                state["rstd"] += 1
                dve.wait_ge(S["rstd"], state["rstd"])
                for p in range(4):
                    for m in range(2):
                        v.scalar_tensor_tensor(out=tmp[:, m * T:m * T + T], in0=bank[4 + p][:, m * T:m * T + T],
                                               scalar=col(gain, 2 * p + m), in1=rstd[:], op0=ALU.mult,
                                               op1=ALU.mult).then_inc(S["dve_step"], told.one("dve_step"))
                        dve.wait_ge(S["dve_step"], told.value("dve_step"))
                    xp = flat(x[:, 2 * p:2 * p + 2, :])
                    v.tensor_tensor(xp, xp, tmp[:], ALU.add).then_inc(S["x_updated"], told.one("x_updated"))
                    dve.wait_ge(S["x_updated"], told.value("x_updated"))

            def residual(last, scale, first_bank=4):
                for p in range(4):
                    if p < 3:
                        dve.wait_ge(S["pair_summed"], 3 * LAYER_ENDS.index(last) + p + 1)
                    else:
                        dve.wait_ge(S["chunk_used"], last)
                    xp = flat(x[:, 2 * p:2 * p + 2, :])
                    v.scalar_tensor_tensor(out=xp, in0=bank[first_bank + p][:, :], scalar=scale, in1=xp,
                                           op0=ALU.mult, op1=ALU.add).then_inc(S["x_updated"], told.one("x_updated"))
                    dve.wait_ge(S["x_updated"], told.value("x_updated"))

            def feed(k):
                b0, before = ffn_at[k], FPAIRS * state["ffn"]
                state["ffn"] += 1

                def convolve(side, i, name, ready):
                    dve.wait_ge(S[ready], i * 2 + 2)
                    for m in range(2):
                        for back in (1, 2):
                            o = acc[:, side, m, back:T]
                            done = name or "dve_step"
                            v.scalar_tensor_tensor(out=o, in0=u_t[:, side, m * T:m * T + T - back],
                                                   scalar=tap(side, i, m, 2 - back), in1=o, op0=ALU.mult,
                                                   op1=ALU.add).then_inc(S[done], told.one(done))
                            dve.wait_ge(S[done], told.value(done))

                def gate_part(i, used):
                    dve.wait_ge(S["chunk_used"], used)
                    dve.wait_ge(S["rstd"], state["rstd"])
                    v.tensor_tensor(u_t[:, 0].rearrange("p (m t) -> p m t", m=2), pairs(0), over(rstd[:], 2),
                                    ALU.mult).then_inc(S["gate_read"], told.one("gate_read"))
                    dve.wait_ge(S["gate_read"], told.value("gate_read"))
                    if k == 0:
                        convolve(0, i, "conv_gate", "taps_gate")

                def val_part(i, used):
                    dve.wait_ge(S["chunk_used"], used)
                    v.tensor_tensor(u_t[:, 1].rearrange("p (m t) -> p m t", m=2), pairs(1), over(rstd[:], 2),
                                    ALU.mult).then_inc(S["val_read"], told.one("val_read"))
                    dve.wait_ge(S["val_read"], told.value("val_read"))
                    val = u_t[:, 1]
                    if k == 0:
                        convolve(1, i, "conv_val", "taps_val")
                        val = flat(acc[:, 1])
                    dve.wait_ge(S["act_gate"], i + (before + 1))
                    v.tensor_tensor(f_t, act_t, val, ALU.mult).then_inc(S["f_ready"], told.one("f_ready"))
                    dve.wait_ge(S["f_ready"], told.value("f_ready"))
                    dve.wait_ge(S["f_hi"], i + (before + 1))
                    v.tensor_tensor(flat(Y_lo[:, 0:2, :]), f_t, flat(Y_hi[:, 0:2, :]).bitcast(F32),
                                    ALU.subtract).then_inc(S["f_lo"], told.one("f_lo"))

                def body(i):
                    for u in range(3):
                        if u == 1:
                            val_part(i, i * 3 + (b0 + 1) if not isinstance(i, int) or i else b0 + 2)
                        if u == 2:
                            gate_part(i + 1, i * 3 + (b0 + 3))
                        m = b0 + 4 + u
                        split(i * 3 + m, m % RING) if not isinstance(i, int) else split(m + 3 * i)

                split(b0 + 2)
                gate_part(0, b0 + 1)
                split(b0 + 3)
                body(0)
                with dve.Fori(1, FPAIRS - 2) as i:
                    per = {"w_lo_dve": 3, "f_lo": 1, "f_ready": 1, "gate_read": 1, "val_read": 1}
                    if k == 0:
                        per.update({"conv_gate": 4, "conv_val": 4})
                    for name in per:
                        told.count[name] -= per[name]
                    told.enter(i, per)
                    body(i)
                    told.leave(FPAIRS - 2)
                body(FPAIRS - 2)
                split(b0 + 34)
                val_part(FPAIRS - 1, b0 + 32 - 1)

            dve.wait_ge(S["par_turned"], 1)
            v.tensor_copy(par[:, 0:512], bank[0][:, :]).then_inc(S["par_ready"], told.one("par_ready"))
            v.tensor_copy(par[:, 512:640], bank[1][:, 0:P]).then_inc(S["par_ready"], told.one("par_ready"))
            dve.wait_ge(S["par_ready"], told.value("par_ready"))
            for b in range(4):
                dve.wait_ge(S["x_turned"], b + 1)
                v.tensor_copy(flat(x[:, 2 * b:2 * b + 2, :]), bank[4 + b][:, :]).then_inc(
                    S["x_updated"], told.one("x_updated"))
                dve.wait_ge(S["x_updated"], told.value("x_updated"))
            split(0)
            split(1)
            dve.wait_ge(S["table_summed"], 1)
            v.tensor_copy(table[0:HPG, 0, T - 1 - SPAN:T], bank[2][0:HPG, T - 1 - SPAN:T]).then_inc(
                S["table_ready"], told.one("table_ready"))
            dve.wait_ge(S["table_ready"], told.value("table_ready"))
            r = DILATION[1]
            v.tensor_copy(table[0:HPG, 1, r - 1:T:r], bank[2][0:HPG, T + r - 1:2 * T:r]).then_inc(
                S["table_ready"], told.one("table_ready"))
            dve.wait_ge(S["table_ready"], told.value("table_ready"))
            r = DILATION[2]
            v.tensor_copy(table[0:HPG, 2, r - 1:T:r], bank[3][0:HPG, r - 1:T:r]).then_inc(
                S["table_ready"], told.one("table_ready"))
            dve.wait_ge(S["table_ready"], told.value("table_ready"))
            x_low("norm_mix_pre")

            taps_left = [(2 * p + m, k) for p in range(NT // 2) for k in range(CONV_W) for m in range(2)]

            def convolve(count):
                for _ in range(min(count, len(taps_left))):
                    t, k = taps_left.pop(0)
                    src, w = c_pad[:, t, k:k + T], col("conv_dw_w", k * NT + t)
                    if k == 0:
                        v.tensor_scalar(conv[:, t, :], src, w, col("conv_dw_b", t), ALU.mult, ALU.add).then_inc(
                            S["tap_done"], told.one("tap_done"))
                    else:
                        dve.wait_ge(S["tap_done"], told.value("tap_done") - 1)
                        v.scalar_tensor_tensor(out=conv[:, t, :], in0=src, scalar=w, in1=conv[:, t, :],
                                               op0=ALU.mult, op1=ALU.add).then_inc(
                            S["tap_done"], told.one("tap_done"))

            for n in range(A_GA):
                split(n + 2)
                if n < A_QKV:
                    p = n // 2
                    dst = glu[:, n % 2, p % 2, :]
                    out_bank(n, dst.rearrange("p (m t) -> p m t", m=2))
                    if n % 2:
                        dve.wait_ge(S["glu_sigmoid"], p + 1)
                        v.tensor_tensor(c_pad[:, 2 * p:2 * p + 2, PAD:PAD + T],
                                        glu[:, 0, p % 2, :].rearrange("p (m t) -> p m t", m=2),
                                        glu[:, 1, p % 2, :].rearrange("p (m t) -> p m t", m=2), ALU.mult).then_inc(
                            S["dve_step"], told.one("dve_step"))
                        dve.wait_ge(S["dve_step"], told.value("dve_step"))
                elif n < A_QKV + 12:
                    j = n - A_QKV
                    dst = q_t if j < 6 else k_t
                    out_bank(n, dst[:, 2 * (j % 6):2 * (j % 6) + 2, :])
                if n >= 2:
                    convolve(9 if n < A_QKV else 10 if n < A_QKV + 12 else 11)
            for it in range(UNITS + 1):
                if it < UNITS:
                    j, i = divmod(it, TT)
                    w = P * (i + 1)
                    dve.wait_ge(S["scores"], it + 1)
                    dve.wait_ge(S["bias_landed"], 16)
                    if it - 1 > 0:
                        dve.wait_ge(S["probs_turned"], it - 1)
                    for gr in range(GROUPS):
                        src = bank[4 + gr // 2][:, gr % 2 * T:gr % 2 * T + w]
                        v.scalar_tensor_tensor(out=s_t[:, it % 2, gr * w:gr * w + w], in0=src, scalar=SCALE,
                                               in1=bias_t[:, gr * HPG + j, T - w:T], op0=ALU.mult,
                                               op1=ALU.add).then_inc(S["scores_read"], told.one("scores_read"))
                    dve.wait_ge(S["scores_read"], GROUPS * (it + 1))
                    v.tensor_reduce(small[:, it % 2:it % 2 + 1], s_t[:, it % 2, 0:GROUPS * w], AX.X, ALU.max,
                                    negate=True).then_inc(S["row_max"], told.one("row_max"))
                    dve.wait_ge(S["row_max"], told.value("row_max"))
                if it:
                    b, w = (it - 1) % 2, GROUPS * P * ((it - 1) % TT + 1)
                    dve.wait_ge(S["exp_done"], it)
                    v.reciprocal(small[:, 4 + b:5 + b], small[:, 2 + b:3 + b]).then_inc(
                        S["dve_step"], told.one("dve_step"))
                    dve.wait_ge(S["dve_step"], told.value("dve_step"))
                    v.tensor_scalar(s_t[:, b, 0:w], s_t[:, b, 0:w], small[:, 4 + b:5 + b], None, ALU.mult).then_inc(
                        S["probs"], told.one("probs"))
                    dve.wait_ge(S["probs"], told.value("probs"))
                if it == 0:
                    assert all(t >= 6 for t, _ in taps_left)
                    convolve(len(taps_left))
                if it < UNITS:
                    n = A_GA + it
                    split(n + 2)
                    out_bank(n, (gate_a if it < 4 else gate_c)[:, 2 * (it % 4):2 * (it % 4) + 2, :])
                if it == 1:
                    diagonals(False)
                if it == 2:
                    dve.wait_ge(S["spread"], 2)
                    v.tensor_tensor(conv, conv, over(bank[3][:, 0:T], NT), ALU.subtract).then_inc(
                        S["centred"], told.one("centred"))
                    dve.wait_ge(S["centred"], told.value("centred"))
                if it == 3:
                    diagonals()
                if it == 4:
                    dve.wait_ge(S["spread"], 3)
                    v.tensor_tensor(conv, conv, over(bank[3][:, 0:T], NT), ALU.mult).then_inc(
                        S["normed"], told.one("normed"))
                    dve.wait_ge(S["normed"], told.value("normed"))
                if it:
                    j, i = divmod(it - 1, TT)
                    dve.wait_ge(S["attn_hi"], it)
                    v.tensor_tensor(Y_lo[:, j, i * P:(i + 1) * P], bank[3][:, 384:512],
                                    Y_hi[:, j, i * P:(i + 1) * P].bitcast(F32), ALU.subtract).then_inc(
                        S["attn_lo"], told.one("attn_lo"))
                    dve.wait_ge(S["attn_lo"], told.value("attn_lo"))
            for n in range(A_AO, A_END):
                split(n + 2)
                if n in (A_AO, A_AO + 1):
                    for k in (0, 1) if n == A_AO else (2, 3):
                        r = PW_ROWS[k]
                        dve.wait_ge(S["silu_hi"], k + 1)
                        v.tensor_tensor(Y_lo[:, 2 * r:2 * r + 2, :], conv[:, 2 * r:2 * r + 2, :],
                                        Y_hi[:, 2 * r:2 * r + 2, :].bitcast(F32), ALU.subtract).then_inc(
                            S["silu_lo"], told.one("silu_lo"))
                if n == A_PW:
                    dve.wait_ge(S["gate_a"], NT)
                    dve.wait_ge(S["chunk_used"], A_PW)
                    for p in range(4):
                        v.tensor_tensor(mixed_a[:, 2 * p:2 * p + 2, :], gate_a[:, 2 * p:2 * p + 2, :],
                                        pairs(4 + p), ALU.mult).then_inc(S["attn_gated"], told.one("attn_gated"))
                    dve.wait_ge(S["attn_gated"], told.value("attn_gated"))
                    dve.wait_ge(S["gate_c"], NT)
                if n >= A_WO - 1 and n < A_WO + 1:
                    dve.wait_ge(S["chunk_used"], A_WO)
                    ps = (0, 1) if n < A_WO else (2, 3)
                    for p in ps:
                        gc, mp = gate_c[:, 2 * p:2 * p + 2, :], mixed_a[:, 2 * p:2 * p + 2, :]
                        v.tensor_tensor(gc, gc, pairs(p), ALU.mult).then_inc(S["dve_step"], told.one("dve_step"))
                        dve.wait_ge(S["dve_step"], told.value("dve_step"))
                        v.tensor_tensor(mp, mp, gc, ALU.add).then_inc(S["mixed"], told.one("mixed"))
                    for p in ps:
                        mp = mixed_a[:, 2 * p:2 * p + 2, :]
                        dve.wait_ge(S["mixed_hi"], p + 1)
                        v.tensor_tensor(X_lo[:, 2 * p:2 * p + 2, :], mp, X_hi[:, 2 * p:2 * p + 2, :].bitcast(F32),
                                        ALU.subtract).then_inc(S["mixed_lo"], told.one("mixed_lo"))
            post_norm("norm_mix_post")
            x_low("norm_ffn_pre")
            feed(0)
            post_norm("norm_ffn_post")
            x_low("ffn1_norm_2")
            feed(1)
            residual(B0, 0.5)
            x_low("mix_norm_2")
            dve_mixer(told, dve, v, split, diagonals, out_bank, state)
            residual(ffn_at[2], 1.0, first_bank=0)
            x_low("ffn2_norm_2")
            feed(2)
            residual(TOTAL, 0.5)
            state["column"] += 1
            dve.wait_ge(S["column"], state["column"])
            v.reciprocal(rcol[:, 0:2], rcol[:, 2:4]).then_inc(S["rcol"], told.one("rcol"))
            dve.wait_ge(S["rcol"], told.value("rcol"))
            for t in range(TT):
                for h in range(2):
                    dve.wait_ge(S["x_back"], 2 * t + h + 1)
                    v.tensor_scalar(out_t[:, t, 512 * h:512 * h + 512], bank[4 + 2 * t + h][:, :],
                                    rcol[:, t:t + 1], None, ALU.mult).then_inc(S["out_ready"], told.one("out_ready"))

        @block.tensor
        def _(pe):
            told = Count()
            state = {"norm": 0, "xg": 0, "diagonals": 0, "rstd": 0, "ffn": 0}

            def split_ready(n):
                pe.wait_ge(S["w_lo_dve"], n + 1)
                pe.wait_ge(S["w_lo_pool"], n + 1)

            def three(o, w, x3, start=False, stop=False):
                (wh, wl), (xh, xl) = w, x3
                pe.matmul(o, wh, xh, start=start, stop=False, skip_group_check=True)
                pe.matmul(o, wh, xl, start=False, stop=False, skip_group_check=True)
                return pe.matmul(o, wl, xh, start=False, stop=stop, skip_group_check=True)

            def by_columns(n, slot, b, source=None, fresh=False):
                split_ready(n)
                hi, lo = source or (X_hi, X_lo)
                for k in range(NT):
                    if fresh:
                        pe.wait_ge(S["xg_lo"], state["xg"] * NT + k + 1)
                    for m in range(2):
                        c = k * 256 + m * P
                        mm = three(bank[b][:, m * T:m * T + T], (w_hi[slot][:, c:c + P], w_lo[slot][:, c:c + P]),
                                   (hi[:, k, :], lo[:, k, :]), start=k == 0 and m == 0, stop=k == NT - 1)
                mm.then_inc(S["chunk_used"], told.one("chunk_used"))
                if fresh:
                    state["xg"] += 1

            def by_tokens(n, slot, b):
                split_ready(n)
                for k in range(NT):
                    wh, wl = (w[slot][:, k * 256:k * 256 + 256] for w in (w_hi, w_lo))
                    for t in range(TT):
                        xh, xl = (h[:, k, t * P:(t + 1) * P] for h in (X_hi, X_lo))
                        mm = three(bank[b][:, t * T:t * T + T], (xh, xl), (wh, wl), start=k == 0 and t == 0,
                                   stop=k == NT - 1)
                mm.then_inc(S["chunk_used"], told.one("chunk_used"))

            def by_rows(n, slot, first_bank, hi, lo, k0, first, last, final=False):
                split_ready(n)
                steps = [(k, o) for k in range(2) for o in range(NT)]
                if final:
                    steps = [(k, 2 * p + m) for p in range(4) for k in range(2) for m in range(2)]
                for at, (k, o) in enumerate(steps):
                    c = k * D + o * P
                    mm = three(bank[first_bank + o // 2][:, o % 2 * T:o % 2 * T + T],
                               (w_hi[slot][:, c:c + P], w_lo[slot][:, c:c + P]), (hi[:, k0 + k, :], lo[:, k0 + k, :]),
                               start=first and k == 0 and o % 2 == 0, stop=last and k == 1)
                    if final and at in (3, 7, 11):
                        mm.then_inc(S["pair_summed"], 1)
                mm.then_inc(S["chunk_used"], told.one("chunk_used"))

            def sum_squares():
                if state["rstd"] > 0:
                    pe.wait_ge(S["rstd"], state["rstd"])
                for p in range(4):
                    pe.wait_ge(S["sq_ready"], 4 * state["norm"] + p + 1)
                    for m in range(2):
                        for t in range(TT):
                            mm = pe.matmul(bank[3][:, 256 + t:257 + t], sq[:, p, m * T + t * P:m * T + t * P + P],
                                           ones[:, 0:1], start=p == 0 and m == 0 and t == 0,
                                           stop=p == 3 and m == 1, skip_group_check=True)
                    mm.then_inc(S["sq_used"], told.one("sq_used"))
                state["norm"] += 1

            def spread(copied=True):
                state["diagonals"] += 1
                state["rstd"] += copied
                pe.wait_ge(S["diagonals"], state["diagonals"])
                for t in range(TT):
                    mm = pe.matmul(bank[3][:, t * P:t * P + P], ones[:, :], diag[:, t, :], start=True, stop=True)
                mm.then_inc(S["spread"], told.one("spread"))

            def feed(k):
                b0, before = ffn_at[k], FPAIRS * state["ffn"]
                state["ffn"] += 1
                by_columns(b0, b0 % RING, 0, fresh=True)
                sum_squares()
                for b in range(4):
                    pe.matmul(bank[4 + b][:, :], zeros_r[:, 0:P], zeros_r[:, :], start=True, stop=False,
                              skip_group_check=True)
                spread()
                by_columns(b0 + 1, (b0 + 1) % RING, 1)

                def body(i):
                    n = i * 3 + (b0 + 2)
                    pe.wait_ge(S["gate_read"], i + (before + 1))
                    by_columns(n, (b0 + 2) % RING, 0)
                    pe.wait_ge(S["val_read"], i + (before + 1))
                    by_columns(n + 1, b0 % RING, 1)
                    pe.wait_ge(S["f_lo"], i + (before + 1))
                    by_rows(n + 2, (b0 + 1) % RING, 4, Y_hi, Y_lo, 0, False, False)

                with pe.Fori(0, FPAIRS - 1) as i:
                    told.enter(i, {"chunk_used": 3})
                    body(i)
                    told.leave(FPAIRS - 1)
                pe.wait_ge(S["f_lo"], before + FPAIRS)
                by_rows(b0 + 32, (b0 + 32) % RING, 4, Y_hi, Y_lo, 0, False, True, final=True)

            def post_norm():
                sum_squares()
                spread()

            pe.wait_ge(S["ident_ready"], 1)
            pe.wait_ge(S["x_landed"], 16)
            for b in range(4):
                for m in range(2):
                    for t in range(TT):
                        mm = pe.transpose(bank[4 + b][:, m * T + t * P:m * T + t * P + P],
                                          x_in[:, t, (2 * b + m) * P:(2 * b + m + 1) * P], ident[:])
                mm.then_inc(S["x_turned"], told.one("x_turned"))
            pe.wait_ge(S["par_landed"], 16 * len(staged))
            for g in range(5):
                mm = pe.transpose(bank[g // 4][:, g % 4 * P:g % 4 * P + P], par_in[:, g, :], ident[:])
            mm.then_inc(S["par_turned"], told.one("par_turned"))
            pe.wait_ge(S["constants"], 1)
            pe.wait_ge(S["rel_landed"], 16)
            for g in range(GROUPS):
                mm = pe.matmul(bank[2 + g // 2][0:HPG, g % 2 * T:g % 2 * T + T],
                               heads[0:BUCKETS, g * HPG:g * HPG + HPG], onehot[0:BUCKETS, :], start=True, stop=True)
            mm.then_inc(S["table_summed"], told.one("table_summed"))
            pe.wait_ge(S["par_ready"], 2)

            for n in range(A_GA):
                b = bank_of[n]
                if reads[n] - 1 > 0:
                    pe.wait_ge(S[f"bank{b}_read"], reads[n] - 1)
                if n == 2:
                    pe.wait_ge(S["table_ready"], GROUPS)
                if n < A_QKV + 12:
                    by_columns(n, n % RING, b, fresh=n == 0)
                else:
                    by_tokens(n, n % RING, b)
                if n == 0:
                    pe.wait_ge(S["table_ready"], GROUPS)
                    sum_squares()
                    spread()
            for it in range(UNITS + 1):
                if it < UNITS:
                    j, i = divmod(it, TT)
                    if it == 0:
                        pe.wait_ge(S["tap_done"], 6 * CONV_W)
                        for b, r in enumerate(all_read(A_GA)):
                            pe.wait_ge(S[f"bank{b}_read"], r)
                    if GROUPS * it > 0:
                        pe.wait_ge(S["scores_read"], GROUPS * it)
                    for gr in range(GROUPS):
                        h = gr * HPG + j
                        mm = pe.matmul(bank[4 + gr // 2][:, gr % 2 * T:gr % 2 * T + P * (i + 1)],
                                       q_t[:, h, i * P:(i + 1) * P], k_t[:, h, 0:P * (i + 1)], start=True, stop=True)
                    mm.then_inc(S["scores"], told.one("scores"))
                    n = A_GA + it
                    pe.wait_ge(S[f"bank{bank_of[n]}_read"], reads[n] - 1)
                    by_columns(n, n % RING, bank_of[n])
                if it == 1:
                    pe.wait_ge(S["tap_done"], NT * CONV_W)
                if it:
                    j, i = divmod(it - 1, TT)
                    pe.wait_ge(S["probs"], it)
                    if it - 1 > 0:
                        pe.wait_ge(S["pT_ready"], it - 1)
                    for b in range(GROUPS * (i + 1)):
                        mm = pe.transpose(bank[6 + b // 4][:, b % 4 * P:b % 4 * P + P],
                                          s_t[:, (it - 1) % 2, b * P:(b + 1) * P], ident[:])
                    mm.then_inc(S["probs_turned"], told.one("probs_turned"))
                if 1 <= it <= 4:
                    if it - 1 > 0:
                        pe.wait_ge(S["attn_lo"], it - 1)
                if it == 1:
                    for t in range(NT):
                        for tt in range(TT):
                            mm = pe.matmul(bank[3][:, 256 + tt:257 + tt], conv[:, t, tt * P:(tt + 1) * P],
                                           ones[:, 0:1], start=t == 0 and tt == 0, stop=t == NT - 1,
                                           skip_group_check=True)
                    mm.then_inc(S["mean_summed"], told.one("mean_summed"))
                if it == 2:
                    spread(False)
                if it == 3:
                    sum_squares()
                if it == 4:
                    spread(False)
                for step, name, count in ((1, "column", 2), (2, "centred", 1), (3, "column", 3), (4, "normed", 1)):
                    if it == step:
                        pe.wait_ge(S[name], count)
                if it:
                    j, i = divmod(it - 1, TT)
                    pe.wait_ge(S["pT_ready"], it)
                    if it - 1 > 0:
                        pe.wait_ge(S["attn_lo"], it - 1)
                    nb = GROUPS * (i + 1)
                    for b in range(nb):
                        gr, kb = divmod(b, i + 1)
                        h = gr * HPG + j
                        mm = pe.matmul(bank[3][:, 384:512], v_t[:, kb, h * HEAD:(h + 1) * HEAD],
                                       pT[:, b * P:(b + 1) * P], start=b == 0, stop=b == nb - 1)
                    mm.then_inc(S["pv_done"], told.one("pv_done"))
            for n in range(A_AO, A_END):
                if n < A_PW:
                    pe.wait_ge(S["attn_lo"], UNITS)
                    r = n - A_AO
                    by_rows(n, n % RING, 4, Y_hi, Y_lo, 2 * r, r == 0, r == 1)
                elif n < A_WO:
                    k = n - A_PW
                    for b, c in enumerate(all_read(A_AO)):
                        pe.wait_ge(S[f"bank{b}_read"], c)
                    pe.wait_ge(S["silu_lo"], k + 1)
                    by_rows(n, n % RING, 0, Y_hi, Y_lo, 2 * PW_ROWS[k], k == 0, k == 3)
                else:
                    r = n - A_WO
                    pe.wait_ge(S["mixed_lo"], r + 1)
                    by_rows(n, n % RING, 4, X_hi, X_lo, 2 * r, r == 0, r == 3, final=r == 3)
            post_norm()
            feed(0)
            post_norm()
            feed(1)
            pe_mixer(told, pe, state, by_columns, by_tokens, by_rows, sum_squares, spread)
            feed(2)
            sum_squares()
            pe.wait_ge(S["xf_ready"], NT)
            for t in range(TT):
                for h in range(2):
                    for f in range(4):
                        mm = pe.transpose(bank[4 + 2 * t + h][:, f * P:(f + 1) * P],
                                          xg[:, 4 * h + f, t * P:(t + 1) * P], ident[:])
                    mm.then_inc(S["x_back"], told.one("x_back"))


_OUTS = [((1, 256, 1024), 'float32')]


def kernel(**inputs):
    import numpy as _np
    import concourse.bacc as _bacc
    from concourse import mybir as _mybir
    from concourse.bass_utils import run_bass_kernel_spmd as _run

    nc = _bacc.Bacc("TRN2", target_bir_lowering=False, num_devices=1)
    arrays, args = {}, {}
    for name in inputs:
        a = _np.ascontiguousarray(inputs[name])
        arrays[f"in_{name}_dram"] = a
        args[name] = nc.dram_tensor(f"in_{name}_dram", a.shape, _mybir.dt.from_np(a.dtype), kind="ExternalInput").ap()
    shape, dtype = _OUTS[0]
    out = nc.dram_tensor("out_0_dram", shape, _mybir.dt.from_np(_np.dtype(dtype)), kind="ExternalOutput").ap()
    scratch = nc.dram_tensor("bias_by_distance", (GROUPS, HPG, 384), F32, kind="Internal").ap()
    shifted = nc.dram_tensor("bias_by_query", (GROUPS * HPG, P, T), F32, kind="Internal").ap()
    block_pair(nc, args, out, scratch, shifted)
    r = _run(nc, [arrays], core_ids=[0])
    return r.results[0]["out_0_dram"]
```
